# Optimizing a Trainium2 kernel written in Bass

```python
import math
import jax, jax.numpy as jnp
from jax import lax
import numpy as np

D_MODEL = 1024
BATCH = 1
SEQ = 512
DEPTH = 1

D_INNER = 2 * D_MODEL
SSM_HEADDIM = 64
SSM_HEADS = D_INNER // SSM_HEADDIM
SSM_GROUPS = 8
SSM_HEADS_PER_GROUP = SSM_HEADS // SSM_GROUPS
SSM_STATE = 128
SSM_CONV = 4
SSM_CHUNK = 128
CONV_DIM = D_INNER + 2 * SSM_GROUPS * SSM_STATE
CONF_DIM = D_MODEL
CONF_KERNEL = 31
N_EXPERTS = 32
TOP_K = 4
D_FF = D_MODEL
SWIGLU_LIMIT = 7.0
SWIGLU_ALPHA = 1.702
MOE_BLOCK = 128
IN_COLS = D_INNER + CONV_DIM + SSM_HEADS + 2 * CONF_DIM + 2 * D_MODEL
EPS = 1e-6

kernel_name = 'hybrid_ssd_conformer_moe_block'

def rms_norm(x, w):
    xf = x.astype(jnp.float32)
    y = xf * lax.rsqrt(jnp.mean(xf * xf, axis=-1, keepdims=True) + EPS)
    return (y * w.astype(jnp.float32)).astype(x.dtype)

def group_rms_norm(y, w, groups):
    b, s, d = y.shape
    yf = y.astype(jnp.float32).reshape(b, s, groups, d // groups)
    yf = yf * lax.rsqrt(jnp.mean(yf * yf, axis=-1, keepdims=True) + EPS)
    return (yf.reshape(b, s, d) * w.astype(jnp.float32)).astype(y.dtype)

def layer_norm(x, w, b):
    xf = x.astype(jnp.float32)
    mu = jnp.mean(xf, axis=-1, keepdims=True)
    var = jnp.mean(jnp.square(xf - mu), axis=-1, keepdims=True)
    y = (xf - mu) * lax.rsqrt(var + EPS)
    return (y * w.astype(jnp.float32) + b.astype(jnp.float32)).astype(x.dtype)

def modulate(h, shift, scale):
    return h * (1.0 + scale[:, None, :]) + shift[:, None, :]

def causal_depthwise_conv(u, w, b):
    width, ch = w.shape
    out = lax.conv_general_dilated(
        u, w[:, None, :].astype(u.dtype), window_strides=(1,), padding=[(width - 1, 0)],
        dimension_numbers=('NWC', 'WIO', 'NWC'), feature_group_count=ch)
    return out + b

def ssd_chunked(xh, dt, a, bm, cm):
    b, s, _, _ = xh.shape
    nc, L, G, R = s // SSM_CHUNK, SSM_CHUNK, SSM_GROUPS, SSM_HEADS_PER_GROUP
    xf = (xh.astype(jnp.float32) * dt[..., None]).reshape(b, nc, L, G, R, SSM_HEADDIM)
    a_dt = (dt * a).reshape(b, nc, L, G, R)
    a_cs = jnp.cumsum(a_dt, axis=2)
    bc = bm.astype(jnp.float32).reshape(b, nc, L, G, SSM_STATE)
    cc = cm.astype(jnp.float32).reshape(b, nc, L, G, SSM_STATE)
    causal = jnp.tril(jnp.ones((L, L), dtype=bool))[None, None, :, :, None, None]
    seg = a_cs[:, :, :, None] - a_cs[:, :, None]
    decay_ls = jnp.exp(jnp.where(causal, seg, -jnp.inf))
    cb = jnp.einsum('bclgn,bcsgn->bclsg', cc, bc)
    y_diag = jnp.einsum('bclsg,bclsgr,bcsgrp->bclgrp', cb, decay_ls, xf)
    decay_to_end = jnp.exp(a_cs[:, :, -1:] - a_cs)
    chunk_states = jnp.einsum('bcsgn,bcsgr,bcsgrp->bcgrpn', bc, decay_to_end, xf)
    chunk_decay = jnp.exp(a_cs[:, :, -1])

    def step(state, inp):
        dec, st = inp
        return state * dec[..., None, None] + st, state

    init = jnp.zeros((b, G, R, SSM_HEADDIM, SSM_STATE), jnp.float32)
    _, states_in = lax.scan(step, init, (jnp.moveaxis(chunk_decay, 1, 0), jnp.moveaxis(chunk_states, 1, 0)))
    states_in = jnp.moveaxis(states_in, 0, 1)
    y_off = jnp.einsum('bclgn,bclgr,bcgrpn->bclgrp', cc, jnp.exp(a_cs), states_in)
    return (y_diag + y_off).reshape(b, s, SSM_HEADS, SSM_HEADDIM).astype(xh.dtype)

def hybrid_mixer(h, w_in, conv_ssm_w, conv_ssm_b, dt_bias, a_log, d_skip, ssm_norm_w, w_ssm_out,
                 conf_dw_w, conf_dw_b, conf_ln_w, conf_ln_b, w_conf_out, w_o):
    b, s, _ = h.shape
    proj = h @ w_in
    cuts = np.cumsum([D_INNER, CONV_DIM, SSM_HEADS, 2 * CONF_DIM]).tolist()
    z, xbc, dt_raw, glu_in, gate_logits = jnp.split(proj, cuts, axis=-1)
    xbc = jax.nn.silu(causal_depthwise_conv(xbc, conv_ssm_w, conv_ssm_b))
    xs, bm, cm = jnp.split(xbc, [D_INNER, D_INNER + SSM_GROUPS * SSM_STATE], axis=-1)
    xh = xs.reshape(b, s, SSM_HEADS, SSM_HEADDIM)
    dt = jax.nn.softplus(dt_raw.astype(jnp.float32) + dt_bias.astype(jnp.float32))
    a = -jnp.exp(a_log.astype(jnp.float32))
    y = ssd_chunked(xh, dt, a, bm.reshape(b, s, SSM_GROUPS, SSM_STATE), cm.reshape(b, s, SSM_GROUPS, SSM_STATE))
    y = (y + d_skip[:, None] * xh).reshape(b, s, D_INNER)
    y = group_rms_norm(y * jax.nn.silu(z), ssm_norm_w, SSM_GROUPS)
    y_a = y @ w_ssm_out
    u_val, u_gate = jnp.split(glu_in, 2, axis=-1)
    u = u_val * jax.nn.sigmoid(u_gate)
    u = causal_depthwise_conv(u, conf_dw_w, conf_dw_b)
    u = jax.nn.silu(layer_norm(u, conf_ln_w, conf_ln_b))
    y_b = u @ w_conf_out
    g_a, g_b = jnp.split(gate_logits, 2, axis=-1)
    merged = jax.nn.sigmoid(g_a) * y_a + jax.nn.sigmoid(g_b) * y_b
    return merged @ w_o

def clamped_swiglu(gu):
    x_glu, x_lin = gu[..., ::2], gu[..., 1::2]
    x_glu = jnp.minimum(x_glu, SWIGLU_LIMIT)
    x_lin = jnp.clip(x_lin, -SWIGLU_LIMIT, SWIGLU_LIMIT)
    return x_glu * jax.nn.sigmoid(SWIGLU_ALPHA * x_glu) * (x_lin + 1.0)

def moe_ffn(h, w_router, b_router, w_gate_up, b_gate_up, w_down, b_down):
    b, s, d = h.shape
    t = b * s
    hf = h.reshape(t, d)
    logits = (hf @ w_router + b_router).astype(jnp.float32)
    top_vals, top_idx = lax.top_k(logits, TOP_K)
    top_w = jax.nn.softmax(top_vals, axis=-1)
    n_assign = t * TOP_K
    e_flat = top_idx.reshape(-1)
    tok_flat = jnp.repeat(jnp.arange(t, dtype=jnp.int32), TOP_K)
    w_flat = top_w.reshape(-1)
    order = jnp.argsort(e_flat)
    e_sorted, tok_sorted, w_sorted = e_flat[order], tok_flat[order], w_flat[order]
    counts = jnp.bincount(e_flat, length=N_EXPERTS)
    starts = jnp.cumsum(counts) - counts
    padded = ((counts + MOE_BLOCK - 1) // MOE_BLOCK) * MOE_BLOCK
    pad_ends = jnp.cumsum(padded)
    pad_starts = pad_ends - padded
    dest = pad_starts[e_sorted] + (jnp.arange(n_assign) - starts[e_sorted])
    n_blocks = (n_assign + MOE_BLOCK - 1) // MOE_BLOCK + N_EXPERTS
    row_tok = jnp.zeros((n_blocks * MOE_BLOCK,), jnp.int32).at[dest].set(tok_sorted)
    row_w = jnp.zeros((n_blocks * MOE_BLOCK,), w_sorted.dtype).at[dest].set(w_sorted)
    block_e = jnp.clip(jnp.searchsorted(pad_ends, jnp.arange(n_blocks) * MOE_BLOCK, side='right'), 0, N_EXPERTS - 1)

    def expert_block(args):
        tok, wt, e = args
        xb = hf[tok]
        hid = clamped_swiglu(xb @ w_gate_up[e] + b_gate_up[e])
        out = hid @ w_down[e] + b_down[e]
        return out * wt[:, None].astype(out.dtype)

    outs = lax.map(expert_block, (row_tok.reshape(n_blocks, MOE_BLOCK), row_w.reshape(n_blocks, MOE_BLOCK), block_e))
    y = jax.ops.segment_sum(outs.reshape(-1, d), row_tok, num_segments=t)
    return y.reshape(b, s, d)

def setup_inputs(seed: int = 0) -> dict:
    key = jax.random.key(seed)
    ks = jax.random.split(key, 32)
    f32 = jnp.float32

    def nrm(k, shape, scale):
        return jax.random.normal(k, shape, f32) * scale

    D = D_MODEL
    gate_offset = jnp.zeros((6 * D,), f32).at[2 * D:3 * D].set(1.0).at[5 * D:6 * D].set(1.0)
    u = jax.random.uniform(ks[8], (DEPTH, SSM_HEADS), f32)
    dt0 = jnp.exp(u * (math.log(0.1) - math.log(0.001)) + math.log(0.001))
    return {
        'x': nrm(ks[0], (BATCH, SEQ, D), 1.0),
        'c': nrm(ks[1], (BATCH, D), 1.0),
        'w_ada': nrm(ks[2], (DEPTH, D, 6 * D), 0.1 * D ** -0.5),
        'b_ada': nrm(ks[3], (DEPTH, 6 * D), 0.02) + gate_offset,
        'norm1_w': 1.0 + nrm(ks[4], (DEPTH, D), 0.02),
        'w_in': nrm(ks[5], (DEPTH, D, IN_COLS), D ** -0.5),
        'conv_ssm_w': nrm(ks[6], (DEPTH, SSM_CONV, CONV_DIM), SSM_CONV ** -0.5),
        'conv_ssm_b': nrm(ks[7], (DEPTH, CONV_DIM), 0.02),
        'dt_bias': dt0 + jnp.log(-jnp.expm1(-dt0)),
        'a_log': jnp.log(jax.random.uniform(ks[9], (DEPTH, SSM_HEADS), f32, 1.0, 16.0)),
        'd_skip': 1.0 + nrm(ks[10], (DEPTH, SSM_HEADS), 0.02),
        'ssm_norm_w': 1.0 + nrm(ks[11], (DEPTH, D_INNER), 0.02),
        'w_ssm_out': nrm(ks[12], (DEPTH, D_INNER, D), D_INNER ** -0.5),
        'conf_dw_w': nrm(ks[13], (DEPTH, CONF_KERNEL, CONF_DIM), CONF_KERNEL ** -0.5),
        'conf_dw_b': nrm(ks[14], (DEPTH, CONF_DIM), 0.02),
        'conf_ln_w': 1.0 + nrm(ks[15], (DEPTH, CONF_DIM), 0.02),
        'conf_ln_b': nrm(ks[16], (DEPTH, CONF_DIM), 0.02),
        'w_conf_out': nrm(ks[17], (DEPTH, CONF_DIM, D), CONF_DIM ** -0.5),
        'w_o': nrm(ks[18], (DEPTH, D, D), D ** -0.5),
        'norm2_w': 1.0 + nrm(ks[19], (DEPTH, D), 0.02),
        'w_router': nrm(ks[20], (DEPTH, D, N_EXPERTS), D ** -0.5),
        'b_router': nrm(ks[21], (DEPTH, N_EXPERTS), 0.01),
        'w_gate_up': nrm(ks[22], (DEPTH, N_EXPERTS, D, 2 * D_FF), D ** -0.5),
        'b_gate_up': nrm(ks[23], (DEPTH, N_EXPERTS, 2 * D_FF), 0.02),
        'w_down': nrm(ks[24], (DEPTH, N_EXPERTS, D_FF, D), D_FF ** -0.5),
        'b_down': nrm(ks[25], (DEPTH, N_EXPERTS, D), 0.02),
        'final_norm_w': 1.0 + nrm(ks[26], (D,), 0.02),
    }

def reference(x, c, w_ada, b_ada, norm1_w, w_in, conv_ssm_w, conv_ssm_b, dt_bias, a_log, d_skip,
              ssm_norm_w, w_ssm_out, conf_dw_w, conf_dw_b, conf_ln_w, conf_ln_b, w_conf_out, w_o,
              norm2_w, w_router, b_router, w_gate_up, b_gate_up, w_down, b_down, final_norm_w):
    c_act = jax.nn.silu(c)
    for l in range(DEPTH):
        mod = c_act @ w_ada[l] + b_ada[l]
        shift1, scale1, gate1, shift2, scale2, gate2 = jnp.split(mod, 6, axis=-1)
        h = modulate(rms_norm(x, norm1_w[l]), shift1, scale1)
        mix = hybrid_mixer(h, w_in[l], conv_ssm_w[l], conv_ssm_b[l], dt_bias[l], a_log[l], d_skip[l],
                           ssm_norm_w[l], w_ssm_out[l], conf_dw_w[l], conf_dw_b[l], conf_ln_w[l],
                           conf_ln_b[l], w_conf_out[l], w_o[l])
        x = x + gate1[:, None, :] * mix
        h = modulate(rms_norm(x, norm2_w[l]), shift2, scale2)
        ffn = moe_ffn(h, w_router[l], b_router[l], w_gate_up[l], b_gate_up[l], w_down[l], b_down[l])
        x = x + gate2[:, None, :] * ffn
    return rms_norm(x, final_norm_w)


_drawn_inputs = setup_inputs


def setup_inputs(seed=0):
    import zlib

    import numpy as np

    out = dict(_drawn_inputs(seed))
    spreads = {}
    factors = {'conf_ln_b': 2.881,
     'b_router': 2.744,
     'b_gate_up': 5.805,
     'b_down': 6.69,
     'final_norm_w': 2.801}
    for name, (base, spread) in spreads.items():
        noise = np.random.default_rng([zlib.crc32(name.encode()), seed]).standard_normal(out[name].shape)
        drawn = base * np.exp(spread * noise) if base else spread * noise
        out[name] = __import__('jax').numpy.asarray(drawn.astype(out[name].dtype))
    for name, factor in factors.items():
        out[name] = (out[name] * factor).astype(out[name].dtype)
    return out
```

```python
from contextlib import ExitStack

import concourse.bass as bass
from concourse import mybir

ALU = mybir.AluOpType
ACT = mybir.ActivationFunctionType
F32 = mybir.dt.float32
I32 = mybir.dt.int32
U32 = mybir.dt.uint32
AX = mybir.AxisListType

P = 128
D = 1024
S = 512
KT = D // P
TT = S // P
G = 8
HG = 4
HD = 64
GW = HG * HD
H = G * HG
DI = G * GW
ST = 128
TAPS = 4
CTAPS = 31
XBC = DI + 2 * G * ST
NE = 32
TOPK = 4
FF = D
SLOTS = 96
MAXI = NE + (S * TOPK) // SLOTS
SPARE = MAXI - NE
SIDE = 1 + -(-SPARE // TT)
MOREMAX = (S - 1) // SLOTS
LIMIT = 7.0
ALPHA = 1.702
EPS = 1e-6
C_Z, C_X, C_B, C_C = 0, DI, 2 * DI, 2 * DI + G * ST
C_DT = DI + XBC
C_VAL = C_DT + H
C_GATE = C_VAL + D
C_GA = C_GATE + D
C_GB = C_GA + D
CW = TAPS * 4 + 4
PW = CW + CTAPS + 1
VPT = 2 * KT


def build(nc, x, c, w_ada, b_ada, norm1_w, w_in, conv_ssm_w, conv_ssm_b, dt_bias, a_log, d_skip,
          ssm_norm_w, w_ssm_out, conf_dw_w, conf_dw_b, conf_ln_w, conf_ln_b, w_conf_out, w_o,
          norm2_w, w_router, b_router, w_gate_up, b_gate_up, w_down, b_down, final_norm_w, out):
    h_rows = nc.dram_tensor("h_rows", [S, D], F32, kind="Internal").ap()
    item_rows = nc.dram_tensor("item_rows", [MAXI * SLOTS, D], F32, kind="Internal").ap()
    decay_rows = nc.dram_tensor("decay_rows", [H, S], F32, kind="Internal").ap()
    mod_rows = nc.dram_tensor("mod_rows", [6 * KT, P], F32, kind="Internal").ap()

    w_in_v = w_in[0].rearrange("(k p) n -> p k n", p=P)
    w_ada_v = w_ada[0].rearrange("(k p) n -> p k n", p=P)
    w_so_v = w_ssm_out[0].rearrange("(k p) n -> p k n", p=P)
    w_co_v = w_conf_out[0].rearrange("(k p) n -> p k n", p=P)
    w_o_v = w_o[0].rearrange("(k p) n -> p k n", p=P)
    x_v = x[0].rearrange("(t p) d -> p t d", p=P)
    out_v = out[0].rearrange("(t p) d -> p t d", p=P)

    with ExitStack() as ctx:
        def sb(name, shape, dt=F32):
            return ctx.enter_context(nc.sbuf_tensor(name, shape, dt))

        def sem(name):
            return ctx.enter_context(nc.semaphore(name))

        ring = sb("ring", [P, 24 * 1024])
        gu = ring[:, 0:16 * 1024].rearrange("p (k n) -> p k n", k=KT)
        dn = ring[:, 16 * 1024:].rearrange("p (k n) -> p k n", k=KT)
        wg = ring[:, 0:8192].rearrange("p (k n) -> p k n", k=KT)
        W_X, W_B, W_C, W_V, W_G, W_Z = 0, 256, 384, 512, 640, 768
        ada = ring[:, 8192:].rearrange("p (s k n) -> p s k n", s=8, k=KT)
        at = 12288
        RW = TAPS - 1 + S
        raw = ring[:, at:at + 4 * RW].rearrange("p (j n) -> p j n", j=4)
        at += 4 * RW
        cacc = ring[:, at:at + 4 * S].rearrange("p (j n) -> p j n", j=4)
        at += 4 * S
        ctan = ring[:, at:at + 4 * S].rearrange("p (j n) -> p j n", j=4)
        at += 4 * S
        cv = ring[:, at:at + 4 * S].rearrange("p (j n) -> p j n", j=4)
        at += 4 * S
        dec = ring[:, at:at + 4 * S].rearrange("p (j n) -> p j n", j=4)
        at += 4 * S
        ugate = ring[:, at:at + S]
        at += S
        upad = ring[:, at:at + CTAPS - 1 + S]
        at += CTAPS - 1 + S
        arow = ring[0:1, at:at + 512]
        at += 512
        assert at <= 24576
        wga = ring[:, 0:1024].rearrange("p (k n) -> p k n", k=KT)
        wgb = ring[:, 1024:2048].rearrange("p (k n) -> p k n", k=KT)
        wya = ring[:, 2048:4096].rearrange("p (k n) -> p k n", k=2 * KT)
        wyb = ring[:, 4096:5120].rearrange("p (k n) -> p k n", k=KT)
        wo = ring[:, 16384:].rearrange("p (k n) -> p k n", k=KT)
        got = ring[:, 0:16 * 1024].rearrange("p (s n) -> p s n", s=16)

        hT = sb("hT", [P, KT, S])
        yT = sb("yT", [P, 2 * KT, S])
        uT = sb("uT", [P, KT, S])
        xs = yT[:, 0:8, :].rearrange("p a b -> p (a b)").rearrange("p (t d) -> p t d", t=TT)
        prow = yT[:, 8:10, :].rearrange("p a b -> p (a b)").rearrange("p (s n) -> p s n", n=P)
        modrow = yT[0:1, 11:15, :].rearrange("p a b -> p (a b)")
        browg = yT[:, 10, :].rearrange("p (s n) -> p s n", s=2)
        x2 = yT[:, 0:8, :].rearrange("p a b -> p (a b)").rearrange("p (t d) -> p t d", t=TT)
        h2 = yT[:, 8:12, :].rearrange("p a b -> p (a b)").rearrange("p (t d) -> p t d", t=2)
        h2T = yT[:, 12:16, :].rearrange("p a b -> p (a b)").rearrange("p (t k n) -> p t k n", t=2, k=KT)
        g1row = uT[:, 0:2, :].rearrange("p a b -> p (a b)")
        a2row = uT[:, 2:4, :].rearrange("p a b -> p (a b)")
        s2row = uT[:, 4:6, :].rearrange("p a b -> p (a b)")
        g2row = uT[:, 6:8, :].rearrange("p a b -> p (a b)")

        ident = sb("ident", [P, P])
        tri = sb("tri", [P, P])
        before = sb("before", [P, P])
        ones = sb("ones", [P, P])
        mean_of = sb("mean_of", [P, P])
        ptab = sb("ptab", [P, G, PW])
        pcur = sb("pcur", [P, PW])
        lnw = sb("lnw", [P, KT])
        lnb = sb("lnb", [P, KT])
        n1w = sb("n1w", [P, KT])
        snw = sb("snw", [P, 2 * KT])
        cact = sb("cact", [P, KT])
        ctmp = sb("ctmp", [P, KT])
        badaT = sb("badaT", [P, VPT])
        mod = sb("mod", [P, VPT])
        a1 = sb("a1", [P, KT])
        bgu = sb("bgu", [P, 2, NE * KT])
        bdn = sb("bdn", [P, NE * KT])
        dsk = sb("dsk", [P, H])
        dt = sb("dt", [P, TT, H])
        adt = sb("adt", [P, TT, H])
        acs = sb("acs", [P, TT, H])
        eacs = sb("eacs", [P, TT, H])
        dte = sb("dte", [P, TT, H])
        cdec = sb("cdec", [P, TT, H])
        acsc = sb("acsc", [P, TT, HG])
        ss = sb("ss", [P, 2 * TT])
        rstd = sb("rstd", [P, 2 * TT])
        mhalf = sb("mhalf", [P, TT])
        epsc = sb("epsc", [P, 1])
        seg = sb("seg", [P, 2, HG, P])
        mm = sb("mm", [P, 2, HG, P])
        cbm = sb("cbm", [P, P])
        dtb = mm[:, 1].rearrange("p h l -> p (h l)")[:, 0:H]
        aneg = mm[:, 1].rearrange("p h l -> p (h l)")[:, H:2 * H]
        wdt = mm[:, 0].rearrange("p h l -> p (h l)")[:, 0:KT * H].rearrange("p (k h) -> p k h", k=KT)
        xb = sb("xb", [P, 2, 3 * P])
        xdt = sb("xdt", [P, 2, HG, HD])
        xdec = sb("xdec", [P, 2, HG, HD])
        xdd = sb("xdd", [P, 2, HG, HD])
        state = sb("state", [P, HG, HD])
        ytmp = sb("ytmp", [P, GW])
        yg = sb("yg", [P, TT, GW])
        zs = sb("zs", [P, TT, GW])
        ztan = sb("ztan", [P, 2, GW])
        c31 = sb("c31", [P, 2, S])
        junk = c31[:, :, :].rearrange("p a b -> p (a b)")

        mT = ring[:, 12288:16384].rearrange("p (k n) -> p k n", k=KT)
        gt = ring[:, 5120:6144].rearrange("p (a n) -> p a n", a=2)
        m1 = ring[:, 6144:7168].rearrange("p (a n) -> p a n", a=2)
        lsq = ring[:, 7168:8192].rearrange("p (a n) -> p a n", a=2)
        lrs = ring[:, 8192:8704]
        lth = ring[:, 8704:9728].rearrange("p (a n) -> p a n", a=2)
        lv = ring[:, 9728:10752].rearrange("p (a n) -> p a n", a=2)

        hTf = hT[:, :, :].rearrange("p a b -> p (a b)")
        xg = hTf[:, 0:1024]
        xT = hTf[:, 1024:1792].rearrange("p (k n) -> p k n", k=KT)
        gsb = hTf[:, 1792:2560].rearrange("p (k n) -> p k n", k=KT)
        lsb = seg[:, :, :, :].rearrange("p a b c -> p (a b c)")[:, 0:768].rearrange("p (k n) -> p k n", k=KT)
        tsb = mm[:, :, :, :].rearrange("p a b c -> p (a b c)")[:, 0:768].rearrange("p (k n) -> p k n", k=KT)
        hid = hTf[:, 2560:3328].rearrange("p (k n) -> p k n", k=KT)
        oT = hTf[:, 3328:4096].rearrange("p (k n) -> p k n", k=KT)
        orow = zs[:, :, :].rearrange("p a b -> p (a b)")
        sel = yg[:, 0:2, :].rearrange("p a b -> p (a b)")[:, 0:TT * SLOTS].rearrange("p (t n) -> p t n", t=TT)
        wr = state[:, :, :].rearrange("p a b -> p (a b)").rearrange("p (k n) -> p k n", k=KT)
        brow = sb("brow", [P, NE])
        lg = cbm[:, :].rearrange("p (t n) -> p t n", t=TT)
        top = sb("top", [P, TT, 8])
        topi = sb("topi", [P, TT, 8], U32)
        topf = sb("topf", [P, TT, 8])
        ntop = sb("ntop", [P, TT])
        ew = sb("ew", [P, TT, TOPK])
        esum = sb("esum", [P, TT])
        tw = sb("tw", [P, TT, TOPK])
        io32 = sb("io32", [P, NE])
        io96 = sb("io96", [P, SLOTS])
        tid = sb("tid", [P, TT])
        ibase = sb("ibase", [P, MAXI + 1])
        oh = ztan[:, :, :].rearrange("p a b -> p (a b)").rearrange("p (t k n) -> p t k n", t=TT, k=TOPK)
        xdecf = xdec[:, :, :, :].rearrange("p a b c -> p (a b c)")
        mask, slot = (xdecf[:, i * 128:(i + 1) * 128].rearrange("p (t n) -> p t n", t=TT) for i in range(2))
        xdtf = xdt[:, :, :, :].rearrange("p a b c -> p (a b c)")
        pos, ci, r1, r2 = (xdtf[:, i * 128:(i + 1) * 128].rearrange("p (t n) -> p t n", t=TT) for i in range(4))
        cnt, more, incl, excl = (xdecf[:, 256 + i * NE:256 + (i + 1) * NE] for i in range(4))
        cmp = junk[0:1, 0:(MAXI + 1 - NE) * NE].rearrange("p (i n) -> p i n", n=NE)
        eidf = xdecf[0:1, 384:384 + MAXI + 1]
        eid = sb("eid", [1, MAXI + 1], I32)
        ntot = sb("ntot", [1, 2], I32)
        slotk = sb("slotk", [P, TT, TOPK])
        slotki = sb("slotki", [P, TT * TOPK], I32)
        rel = sb("rel", [P, TT])
        tok = sb("tok", [P, 1], I32)
        fn = g1row
        sqj = sb("sqj", [P, GW])

        ps = ctx.enter_context(nc.psum_tensor("ps", [P, 8, 512], F32))

        x_in, rows_in, bc_in, wdt_in, wx_in, wbc_in, wvg_in, wz_in = map(sem, 'x_in rows_in bc_in wdt_in wx_in wbc_in wvg_in wz_in'.split())
        dec_in, side_out, const_ok, xn_ok, prT_ok, par_ok, cact_t, cact_ok = map(sem, 'dec_in side_out const_ok xn_ok prT_ok par_ok cact_t cact_ok'.split())
        ada_ok, mod_ok, a1_ok, xT_ok, hT_ok, dtr_ok, acs_pe, proj_x = map(sem, 'ada_ok mod_ok a1_ok xT_ok hT_ok dtr_ok acs_pe proj_x'.split())
        proj_bc, proj_vg, proj_z, raw_x, raw_bc, conv_ok, ctan_ok, cv_ok = map(sem, 'proj_bc proj_vg proj_z raw_x raw_bc conv_ok ctan_ok cv_ok'.split())
        pcur_ok, acsc_ok, T_ok, CB_ok, Y_ok, ST_ok, YT_ok, ada_l = map(sem, 'pcur_ok acsc_ok T_ok CB_ok Y_ok ST_ok YT_ok ada_l'.split())
        xb_ok, seg_ok, exp_ok, cbm_ok, m_ok, xdt_ok, xdec_ok, xdd_ok = map(sem, 'xb_ok seg_ok exp_ok cbm_ok m_ok xdt_ok xdec_ok xdd_ok'.split())
        state_ok, y_ok, ysq_ok, yrms_ok, yrstd_ok, ysc_ok, yT_ok, gtan_ok = map(sem, 'state_ok y_ok ysq_ok yrms_ok yrstd_ok ysc_ok yT_ok gtan_ok'.split())
        glu_ok, c31_ok, ztan_ok, zs_ok, pads_ok, mw_ga, mw_gb, mw_ya = map(sem, 'glu_ok c31_ok ztan_ok zs_ok pads_ok mw_ga mw_gb mw_ya'.split())
        mw_yb, wo_in, arow_in, modT_pe, arow_ok, modrow_out, brow_in, row_ok = map(sem, 'mw_yb wo_in arow_in modT_pe arow_ok modrow_out brow_in row_ok'.split())
        once_in, fn_in, mean_pe, cen_ok, lsq_ok, var_pe, lsd_ok, lrs_ok = map(sem, 'once_in fn_in mean_pe cen_ok lsq_ok var_pe lsd_ok lrs_ok'.split())
        lnm_ok, lnv_ok, lth_ok, u_ok, ga_pe, gb_pe, ya_pe, yb_pe = map(sem, 'lnm_ok lnv_ok lth_ok u_ok ga_pe gb_pe ya_pe yb_pe'.split())
        gat_ok, gbt_ok, mrg_ok, o_pe, x2_ok, x2_in, h2_ok, h2T_pe = map(sem, 'gat_ok gbt_ok mrg_ok o_pe x2_ok x2_in h2_ok h2T_pe'.split())
        h2T_ok, lg_pe, lg_ok, rt_ok, exw_ok, rank_pe, ntop_ok, mask_ok = map(sem, 'h2T_ok lg_pe lg_ok rt_ok exw_ok rank_pe ntop_ok mask_ok'.split())
        tab_ok, sel_ok, tok_pe, tok_ok, xg_in, tx_pe, xTi_ok, gu_pe = map(sem, 'tab_ok sel_ok tok_pe tok_ok xg_in tx_pe xTi_ok gu_pe'.split())
        act_ok, tan_ok, hid_ok, dn_pe, oT_ok, to_pe, orow_ok, orow_out = map(sem, 'act_ok tan_ok hid_ok dn_pe oT_ok to_pe orow_ok orow_out'.split())
        fin_ok, out_done, sq_ok, rms_ok, rstd_ok, time_dve, time_act = map(sem, 'fin_ok out_done sq_ok rms_ok rstd_ok time_dve time_act'.split())
        ada_in = [sem(f"ada_in{i}") for i in range(8)]
        hrow_out = [sem(f"hrow_out{i}") for i in range(2)]
        gu_in = [sem(f"gu_in{k}") for k in range(KT)]
        dn_in = [sem(f"dn_in{k}") for k in range(KT)]
        got_in = [sem(f"got_in{t}") for t in range(TT)]

        def ch(c):
            return slice(c * P, (c + 1) * P)

        def y_after(g, c):
            return 14 * g + 2 + 4 * c

        LG_BANK = (6, 7, 0, 1)
        STATE_AFTER = (1, 3, 5)


        def plain(engine, sem_, value, other, count):
            if not isinstance(value, int):
                nc.lower_val(value, engines=[engine.engine])
            engine.wait_ge(other, count)
            engine.wait_ge(sem_, value)

        block = ctx.enter_context(nc.Block())

        @block.sync
        def _(sp):
            sp.dma_start(xs, x_v).then_inc(x_in, 16)
            sp.dma_start(wdt, w_in_v[:, :, C_DT:C_DT + H]).then_inc(wdt_in, 16)
            for s in range(8):
                sp.dma_start(ada[:, s], w_ada_v[:, :, s * 256:(s + 1) * 256]).then_inc(ada_in[s], 16)

            def load_x(g):
                sp.dma_start(wg[:, :, W_X:W_X + 256], w_in_v[:, :, bass.ds(g * 256 + C_X, 256)]).then_inc(wx_in, 16)

            def load_bc(g):
                sp.dma_start(wg[:, :, W_B:W_B + P], w_in_v[:, :, bass.ds(g * P + C_B, P)]).then_inc(wbc_in, 16)
                sp.dma_start(wg[:, :, W_C:W_C + P], w_in_v[:, :, bass.ds(g * P + C_C, P)]).then_inc(wbc_in, 16)

            def load_vg(g):
                sp.dma_start(wg[:, :, W_V:W_V + P], w_in_v[:, :, bass.ds(g * P + C_VAL, P)]).then_inc(wvg_in, 16)
                sp.dma_start(wg[:, :, W_G:W_G + P], w_in_v[:, :, bass.ds(g * P + C_GATE, P)]).then_inc(wvg_in, 16)

            def load_z(g):
                sp.dma_start(wg[:, :, W_Z:W_Z + 256], w_in_v[:, :, bass.ds(g * 256 + C_Z, 256)]).then_inc(wz_in, 16)

            def load_dec(g):
                sp.dma_start(dec, decay_rows[bass.ds(g * HG, HG), :].partition_broadcast(P)).then_inc(dec_in, 16)

            def load_arow(g):
                sp.dma_start(arow, b_ada[0:1, bass.ds(g * 512 + VPT * P, 512)]).then_inc(arow_in, 16)

            def store_arow(g):
                sp.wait_ge(arow_ok, g + 1)
                sp.dma_start(mod_rows[bass.ds(4 * g + VPT, 4), :].rearrange("a b -> (a b)").unsqueeze(0), arow).then_inc(modrow_out, 16)

            def load_ada(g):
                for s in range(2):
                    sp.dma_start(ada[:, s], w_ada_v[:, :, bass.ds(g * 512 + (VPT + 2 * s) * P, 256)]).then_inc(ada_in[s], 16)

            load_x(0)
            load_bc(0)
            load_vg(0)
            load_z(0)
            sp.wait_ge(ada_ok, 8)
            load_ada(0)
            load_arow(0)
            sp.wait_ge(proj_x, 2)
            load_x(1)
            sp.wait_ge(proj_bc, 2)
            load_bc(1)
            sp.wait_ge(time_dve, 6)
            sp.dma_start(decay_rows, junk[0:H, 0:S]).then_inc(side_out, 16)
            sp.wait_ge(proj_vg, 2)
            load_vg(1)
            sp.wait_ge(side_out, 16)
            load_dec(0)
            sp.wait_ge(proj_z, 2)
            load_z(1)

            def follow(g):
                sp.wait_ge(proj_x, 2 * (g + 2))
                load_x(g + 2)
                sp.wait_ge(proj_bc, 2 * (g + 2))
                load_bc(g + 2)
                sp.wait_ge(proj_vg, 2 * (g + 2))
                load_vg(g + 2)
                sp.wait_ge(x_in, 16)
                sp.wait_ge(proj_z, 2 * (g + 2))
                load_z(g + 2)

            def load_merge(m):
                if not isinstance(m, int):
                    sp.wait_ge(ga_pe, m)
                sp.dma_start(wga, w_in_v[:, :, bass.ds(m * P + C_GA, P)]).then_inc(mw_ga, 16)
                if not isinstance(m, int):
                    sp.wait_ge(gb_pe, m)
                sp.dma_start(wgb, w_in_v[:, :, bass.ds(m * P + C_GB, P)]).then_inc(mw_gb, 16)
                if not isinstance(m, int):
                    sp.wait_ge(x_in, 16)
                    sp.wait_ge(ya_pe, m)
                sp.dma_start(wya, w_so_v[:, :, bass.ds(m * P, P)]).then_inc(mw_ya, 16)
                if not isinstance(m, int):
                    sp.wait_ge(yb_pe, m)
                sp.dma_start(wyb, w_co_v[:, :, bass.ds(m * P, P)]).then_inc(mw_yb, 16)

            def follow_rest(g):
                sp.wait_ge(seg_ok, 16 * (g + 1))
                load_dec(g + 1)
                if isinstance(g, int):
                    sp.wait_ge(proj_z, 2 * G)
                    load_merge(0)
                sp.wait_ge(ada_l, 2 * (g + 1))
                load_ada(g + 1)
                store_arow(g)
                sp.wait_ge(modrow_out, 16 * (g + 1))
                load_arow(g + 1)

            spare = item_rows[NE * SLOTS:, :].rearrange("(s p) d -> p s d", p=SLOTS)
            for s in range(0, SPARE, TT):
                n = min(TT, SPARE - s)
                sp.dma_start(spare[:, s:s + n, :], hT[0:SLOTS, 0:2 * n, :].rearrange("p a b -> p (a b)")
                             .rearrange("p (s d) -> p s d", d=D)).then_inc(side_out, 16)
            with sp.Fori(0, G - 2) as g:
                follow(g)
                follow_rest(g)
            follow_rest(G - 2)

            sp.wait_ge(YT_ok, 2 * G)
            sp.wait_ge(c31_ok, (CTAPS + 1) * G)
            sp.wait_ge(y_ok, y_after(G - 1, 3))
            store_arow(G - 1)
            sp.wait_ge(modrow_out, 16 * G)
            sp.dma_start(wo, w_o_v).then_inc(wo_in, 16)
            with sp.Fori(1, KT) as m:
                load_merge(m)

            def mod_row(a):
                return mod_rows[a * KT:(a + 1) * KT, :].rearrange("a b -> (a b)").partition_broadcast(P)

            sp.wait_ge(ya_pe, KT)
            sp.dma_start(x2, x_v).then_inc(x2_in, 16)
            sp.dma_start(wr, w_router[0].rearrange("(k p) n -> p k n", p=P)).then_inc(once_in, 16)
            sp.wait_ge(yb_pe, KT)
            sp.wait_ge(modrow_out, 16 * G)
            sp.dma_start(g1row, mod_row(2)).then_inc(brow_in, 16)
            sp.dma_start(a2row, mod_row(4)).then_inc(brow_in, 16)
            sp.dma_start(s2row, mod_row(3)).then_inc(brow_in, 16)
            sp.dma_start(g2row, mod_row(5)).then_inc(brow_in, 16)
            sp.dma_start(h2[:, 0, :], norm2_w[0].partition_broadcast(P)).then_inc(brow_in, 16)

            def load_gu(e, k):
                sp.dma_start(gu[:, k, :], w_gate_up[0][bass.ds(e, 1), k * P:(k + 1) * P, :].rearrange("a p n -> (a p) n"))\
                    .then_inc(gu_in[k], 16)

            def load_dn(e, k):
                sp.dma_start(dn[:, k, :], w_down[0][bass.ds(e, 1), k * P:(k + 1) * P, :].rearrange("a p n -> (a p) n"))\
                    .then_inc(dn_in[k], 16)

            sp.wait_ge(mrg_ok, 3 * KT)
            for k in range(6):
                load_gu(0, k)
            for t in range(TT):
                sp.wait_ge(h2_ok, 2 * (t + 1))
                sp.dma_start(h_rows[ch(t), :], h2[:, t % 2, :]).then_inc(hrow_out[t % 2], 16)
                if t == 0:
                    sp.wait_ge(o_pe, 2 * TT)
                    for k in range(6, KT):
                        load_gu(0, k)
                    for k in range(KT):
                        load_dn(0, k)
            sp.wait_ge(x2_ok, 4 * TT)
            sp.dma_start(fn, final_norm_w.partition_broadcast(P)).then_inc(fn_in, 16)
            sp.wait_ge(tab_ok, 4)
            items = sp.value_load(ntot[0:1, 0:1], min_val=NE, max_val=MAXI)
            with sp.Fori(1, items) as i:
                e = sp.value_load(eid[0:1, bass.ds(i, 1)], min_val=0, max_val=NE - 1)
                for k in range(KT):
                    sp.wait_ge(gu_pe, 9 * (i - 1) + (k + 1 if k < KT - 1 else 9))
                    load_gu(e, k)
                for k in range(KT):
                    sp.wait_ge(dn_pe, 8 * (i - 1) + k + 1)
                    load_dn(e, k)
            for t in range(TT):
                sp.wait_ge(fin_ok, 6 * t + 6)
                sp.dma_start(out_v[:, t, :], x2[:, t, :]).then_inc(out_done, 16)
            sp.wait_ge(out_done, 16 * TT)

        @block.gpsimd
        def _(pool):
            nc.gpsimd.memset(mhalf[:, :], -0.5).then_inc(const_ok, 1)
            nc.gpsimd.memset(epsc[:, :], EPS).then_inc(const_ok, 1)
            nc.gpsimd.memset(mean_of[:, :], 1.0 / D).then_inc(const_ok, 1)
            nc.gpsimd.memset(ones[:, :], 1.0).then_inc(const_ok, 1)
            pool.wait_ge(const_ok, 4)
            nc.gpsimd.affine_select(out=ident[:, :], in_=ones[:, :], compare_op=ALU.is_equal, fill=0.0, base=0,
                                    pattern=[[1, P]], channel_multiplier=-1).then_inc(const_ok, 1)
            nc.gpsimd.affine_select(out=tri[:, :], in_=ones[:, :], compare_op=ALU.is_ge, fill=0.0, base=0,
                                    pattern=[[1, P]], channel_multiplier=-1).then_inc(const_ok, 1)
            nc.gpsimd.affine_select(out=before[:, :], in_=ones[:, :], compare_op=ALU.is_gt, fill=0.0, base=0,
                                    pattern=[[1, P]], channel_multiplier=-1).then_inc(const_ok, 1)
            fl = dict(allow_small_or_imprecise_dtypes=True)
            nc.gpsimd.iota(io32[:, :], [[1, NE]], base=0, channel_multiplier=0, **fl).then_inc(const_ok, 1)
            nc.gpsimd.iota(io96[:, :], [[1, SLOTS]], base=0, channel_multiplier=0, **fl).then_inc(const_ok, 1)
            nc.gpsimd.iota(tid[:, :], [[P, TT]], base=0, channel_multiplier=1, **fl).then_inc(const_ok, 1)
            nc.gpsimd.iota(ibase[:, :], [[SLOTS, MAXI + 1]], base=0, channel_multiplier=0, **fl).then_inc(const_ok, 1)

            def rstd_of(lo, n, count, eps, ready, ready_at, mid, mid_at, done):
                pool.wait_ge(ready, ready_at)
                nc.gpsimd.tensor_scalar(ss[:, lo:lo + n], ss[:, lo:lo + n], 1.0 / count, eps, ALU.mult, ALU.add).then_inc(mid, 1)
                pool.wait_ge(mid, mid_at)
                nc.gpsimd.tensor_tensor(rstd[:, lo:lo + n], ss[:, lo:lo + n], mhalf[:, 0:n], ALU.pow).then_inc(done, 1)

            rstd_of(0, TT, D, EPS, sq_ok, TT, rms_ok, 1, rstd_ok)
            pool.wait_ge(time_dve, 3)
            pool.wait_ge(time_act, 6)
            pool.wait_ge(bc_in, 64)

            def heads(t, g, c=None):
                v = t[:, c, bass.ds(g * HG, HG)] if c is not None else t[:, bass.ds(g * HG, HG)]
                return v.unsqueeze(2).to_broadcast([P, HG, HD])

            def scaled(g, c, first):
                xc = xb[:, c % 2, 0:GW].rearrange("p (h d) -> p h d", h=HG)
                pool.wait_ge(xb_ok, 4 * g + c + 1)
                if not first or c >= 2:
                    pool.wait_ge(Y_ok, 4 * g + c - 1)
                nc.gpsimd.tensor_tensor(xdt[:, c % 2], xc, heads(dt, g, c), ALU.mult).then_inc(xdt_ok, 1)
                if c < 3:
                    if not first or c == 2:
                        pool.wait_ge(ST_ok, 3 * g + (c == 2))
                    pool.wait_ge(xdt_ok, 4 * g + c + 1)
                    nc.gpsimd.tensor_tensor(xdec[:, c % 2], xdt[:, c % 2], heads(dte, g, c), ALU.mult).then_inc(xdec_ok, 1)
                if not first or c >= 2:
                    plain(nc.gpsimd, y_ok, y_after(g, c - 2) if c >= 2 else 14 * g - 4 + 4 * c, const_ok, 11)
                nc.gpsimd.tensor_tensor(xdd[:, c % 2], xc, heads(dsk, g), ALU.mult).then_inc(xdd_ok, 1)

            def group(g, first=False):
                scaled(g, 0, first)
                scaled(g, 1, first)
                scaled(g, 2, first)
                if not first:
                    plain(nc.gpsimd, ysc_ok, 4 * g - 2, const_ok, 11)
                rstd_of(TT, 2, GW, 4 * EPS, ysq_ok, 4 * g + 2, yrms_ok, 2 * g + 1, yrstd_ok)
                scaled(g, 3, first)
                if not first:
                    plain(nc.gpsimd, ysc_ok, 4 * g, const_ok, 11)
                rstd_of(TT + 2, 2, GW, 4 * EPS, ysq_ok, 4 * g + 4, yrms_ok, 2 * g + 2, yrstd_ok)

            group(0, first=True)
            with pool.Fori(1, G) as g:
                group(g)

            for t in range(TT):
                rstd_of(t, 1, D, EPS, sq_ok, TT + t + 1, rms_ok, t + 2, rstd_ok)

            pool.wait_ge(tab_ok, 4)
            items = pool.value_load(ntot[0:1, 0:1], min_val=NE, max_val=MAXI)

            def gather(i, first=False):
                plain(nc.gpsimd, tok_ok, i + 1, const_ok, 11)
                if not first:
                    pool.wait_ge(tx_pe, i)
                nc.gpsimd.indirect_dma_start(
                    xg[0:SLOTS, :], None, h_rows,
                    bass.IndirectOffsetOnAxis(ap=tok[0:SLOTS, :].bitcast(U32), axis=0)).then_inc(xg_in, 16)

            for s in range(2):
                pool.wait_ge(hrow_out[s], 32)
            pool.wait_ge(side_out, 16 * SIDE)
            gather(0, first=True)
            with pool.Fori(1, items + 1) as i:
                gather(i)

            pool.wait_ge(orow_out, 16 * items)
            plain(nc.gpsimd, dn_pe, 8 * items, const_ok, 11)
            for t in range(TT):
                for k in range(TOPK):
                    s = t * TOPK + k
                    nc.gpsimd.indirect_dma_start(
                        got[:, s, :], None, item_rows,
                        bass.IndirectOffsetOnAxis(ap=slotki[:, s:s + 1].bitcast(U32), axis=0)).then_inc(got_in[t], 16)
            for t in range(TT):
                rstd_of(t, 1, D, EPS, sq_ok, 2 * TT + t + 1, rms_ok, TT + t + 2, rstd_ok)

        @block.scalar
        def _(act):
            rows = [
                (prow[:, 0, :], conv_ssm_w[0].rearrange("k (t n) -> (k t) n", n=P)),
                (prow[:, 1, :], conf_dw_w[0].rearrange("k (j n) -> (k j) n", n=P)[0:P, :]),
                (prow[0:CTAPS * G - P, 2, :], conf_dw_w[0].rearrange("k (j n) -> (k j) n", n=P)[P:CTAPS * G, :]),
                (prow[0:32, 3, :], conv_ssm_b[0].rearrange("(t n) -> t n", n=P)),
                (prow[32:40, 3, :], conf_dw_b[0].rearrange("(t n) -> t n", n=P)),
                (prow[40:48, 3, :], conf_ln_w[0].rearrange("(t n) -> t n", n=P)),
                (prow[48:56, 3, :], conf_ln_b[0].rearrange("(t n) -> t n", n=P)),
                (prow[56:64, 3, :], norm1_w[0].rearrange("(t n) -> t n", n=P)),
                (prow[64:80, 3, :], ssm_norm_w[0].rearrange("(t n) -> t n", n=P)),
                (prow[0:VPT, 4, :], b_ada[0, 0:VPT * P].rearrange("(t n) -> t n", n=P)),
                (prow[:, 5:7, :], b_down[0].rearrange("e (t n) -> (e t) n", n=P).rearrange("(s p) n -> p s n", p=P)),
                (browg, b_gate_up[0].rearrange("e (m n) -> (e m) n", n=256).rearrange("(s p) n -> p s n", p=P)),
            ]
            act.dma_start(prow[0:KT, 7, :], c[0].rearrange("(t n) -> t n", n=P)).then_inc(once_in, 16)
            for dst, src in rows:
                act.dma_start(dst, src).then_inc(rows_in, 16)
            for dst, src in ((dtb, dt_bias[0]), (aneg, a_log[0]), (dsk[:, :], d_skip[0]), (brow[:, :], b_router[0])):
                act.dma_start(dst, src.partition_broadcast(P)).then_inc(bc_in, 16)

            act.wait_ge(par_ok, 1)
            nc.scalar.activation(cact[:, :], ctmp[:, :], ACT.Tanh).then_inc(cact_t, 1)
            act.wait_ge(x_in, 16)
            for t in range(TT):
                if t:
                    act.wait_ge(sq_ok, t)
                nc.scalar.activation(junk, xs[:, t, :], ACT.Square, accum_out=ss[:, t:t + 1]).then_inc(sq_ok, 1)
            for b in range(4):
                act.wait_ge(ada_ok, 2 * b + 2)
                nc.scalar.activation(modrow[0:1, b * 512:(b + 1) * 512], ps[0:1, b, :], ACT.Copy).then_inc(cact_t, 1)
            act.wait_ge(a1_ok, 1)
            for k in range(KT):
                act.wait_ge(xT_ok, k + 1)
                nc.scalar.activation(hT[:, k, :], ps[:, k % 4, :], ACT.Identity, bias=mod[:, k:k + 1],
                                     scale=a1[:, k:k + 1]).then_inc(hT_ok, 1)

            def raw_xs(g, first=False):
                for j in range(2):
                    act.wait_ge(proj_x, 2 * g + j + 1)
                    if not first:
                        act.wait_ge(conv_ok, 16 * g - 8)
                    else:
                        act.wait_ge(pads_ok, 2)
                    nc.scalar.activation(raw[:, j, TAPS - 1:], ps[:, j, :], ACT.Copy).then_inc(raw_x, 1)

            def raw_bcs(g, first=False):
                for j in range(2):
                    act.wait_ge(proj_bc, 2 * g + j + 1)
                    if not first:
                        act.wait_ge(conv_ok, 16 * g)
                    nc.scalar.activation(raw[:, 2 + j, TAPS - 1:], ps[:, 2 + j, :], ACT.Copy).then_inc(raw_bc, 1)

            def gate_tanh(g, first=False):
                act.wait_ge(proj_vg, 2 * g + 2)
                if not first:
                    act.wait_ge(glu_ok, g)
                nc.scalar.activation(ugate, ps[:, 1, :], ACT.Tanh, scale=0.5).then_inc(gtan_ok, 1)

            def z_tanh(g, b, first=False):
                act.wait_ge(proj_z, 2 * g + b + 1)
                if not first or b:
                    act.wait_ge(zs_ok, 2 * g + b)
                nc.scalar.activation(ztan[:, :, :].rearrange("p a b -> p (a b)"), ps[:, 2 + b, :], ACT.Tanh,
                                     scale=0.5).then_inc(ztan_ok, 1)

            def conv_tanh(g, first=False):
                for j in range(4):
                    act.wait_ge(conv_ok, 16 * g + (8 if j < 2 else 16))
                    if not first:
                        act.wait_ge(cv_ok, 4 * g)
                    nc.scalar.activation(ctan[:, j, :], cacc[:, j, :], ACT.Tanh).then_inc(ctan_ok, 1)

            def tokens_first(g, c, first):
                act.wait_ge(T_ok, 4 * g + c + 1)
                if not first or c >= 2:
                    act.wait_ge(xdd_ok, 4 * g + c - 1)
                if c >= 2:
                    act.wait_ge(ST_ok, 3 * g + c - 1)
                elif not first:
                    act.wait_ge(ST_ok, 3 * g)
                nc.scalar.activation(xb[:, c % 2, :], ps[:, 4, 0:3 * P], ACT.Copy).then_inc(xb_ok, 1)

            def decay_exp(g, c):
                act.wait_ge(seg_ok, 16 * g + 4 * c + 4)
                v = seg[:, c % 2].rearrange("p h l -> p (h l)")
                nc.scalar.activation(v, v, ACT.Exp).then_inc(exp_ok, 1)

            def square_y(g, c, first):
                act.wait_ge(y_ok, y_after(g, c))
                if not first or c:
                    act.wait_ge(ysq_ok, 4 * g + c)
                if not first:
                    act.wait_ge(yrstd_ok, 2 * g - 1 + c // 2)
                nc.scalar.activation(sqj[:, :], yg[:, c, :], ACT.Square, accum_out=ss[:, TT + c:TT + c + 1]).then_inc(ysq_ok, 1)

            def y_turned(g, r):
                act.wait_ge(YT_ok, 2 * g + r + 1)
                for i in range(2):
                    nc.scalar.activation(yT[:, bass.ds(2 * g + i, 1), 2 * r * P:2 * (r + 1) * P].rearrange("p a b -> p (a b)"),
                                         ps[:, 7, i * 256:(i + 1) * 256], ACT.Identity,
                                         scale=snw[:, bass.ds(2 * g + i, 1)]).then_inc(yT_ok, 1)

            raw_xs(0, first=True)
            act.wait_ge(time_dve, 2)
            f = "p t h -> p (t h)"
            nc.scalar.activation(acs[:, :, :].rearrange(f), adt[:, :, :].rearrange(f), ACT.Exp, scale=-1.0).then_inc(time_act, 1)
            act.wait_ge(time_act, 1)
            nc.scalar.activation(eacs[:, :, :].rearrange(f), acs[:, :, :].rearrange(f), ACT.Ln, bias=1.0).then_inc(time_act, 1)
            act.wait_ge(bc_in, 64)
            nc.scalar.activation(aneg, aneg, ACT.Exp).then_inc(time_act, 1)
            act.wait_ge(acs_pe, 1)
            act.wait_ge(time_dve, 5)
            nc.scalar.activation(eacs[:, :, :].rearrange(f), ps[:, 5, 0:P], ACT.Exp).then_inc(time_act, 1)
            nc.scalar.activation(cdec[:, :, :].rearrange(f), ps[:, 5, P:2 * P], ACT.Exp).then_inc(time_act, 1)
            act.wait_ge(time_dve, 7)
            nc.scalar.activation(dte[:, :, :].rearrange(f), dte[:, :, :].rearrange(f), ACT.Exp).then_inc(time_act, 1)
            raw_bcs(0, first=True)
            gate_tanh(0, first=True)
            z_tanh(0, 0, first=True)
            z_tanh(0, 1, first=True)
            conv_tanh(0, first=True)

            def group(g, first=False, last=False):
                if not last:
                    raw_xs(g + 1)
                if not first:
                    y_turned(g - 1, 1)
                tokens_first(g, 0, first)
                decay_exp(g, 0)
                if not last:
                    raw_bcs(g + 1)
                decay_exp(g, 1)
                tokens_first(g, 1, first)
                square_y(g, 0, first)
                if not last:
                    gate_tanh(g + 1)
                decay_exp(g, 2)
                if not last:
                    conv_tanh(g + 1)
                tokens_first(g, 2, first)
                square_y(g, 1, first)
                if not last:
                    z_tanh(g + 1, 0)
                decay_exp(g, 3)
                y_turned(g, 0)
                tokens_first(g, 3, first)
                square_y(g, 2, first)
                square_y(g, 3, first)
                if not last:
                    z_tanh(g + 1, 1)

            group(0, first=True)
            with act.Fori(1, G - 1) as g:
                group(g)
            group(G - 1, last=True)
            y_turned(G - 1, 1)

            def gates(m):
                act.wait_ge(ga_pe, m + 1)
                if not isinstance(m, int):
                    act.wait_ge(mrg_ok, 3 * m - 2)
                nc.scalar.activation(gt[:, 0, :], ps[:, 0, :], ACT.Tanh, scale=0.5).then_inc(gat_ok, 1)
                act.wait_ge(gb_pe, m + 1)
                if not isinstance(m, int):
                    act.wait_ge(mrg_ok, 3 * m - 1)
                nc.scalar.activation(gt[:, 1, :], ps[:, 1, :], ACT.Tanh, scale=0.5).then_inc(gbt_ok, 1)

            for j in range(KT):
                act.wait_ge(cen_ok, j + 1)
                if j >= 2:
                    act.wait_ge(var_pe, j - 1)
                nc.scalar.activation(lsq[:, j % 2, :], uT[:, j, :], ACT.Square).then_inc(lsq_ok, 1)
                if j == 1:
                    gates(0)
            act.wait_ge(var_pe, KT)
            nc.scalar.activation(lrs, ps[:, 5, :], ACT.Sqrt, bias=epsc[:, 0:1]).then_inc(lsd_ok, 1)
            for j in range(KT):
                act.wait_ge(lnm_ok, j + 1)
                if j >= 2:
                    act.wait_ge(u_ok, j - 1)
                nc.scalar.activation(lth[:, j % 2, :], uT[:, j, :], ACT.Tanh, bias=lnb[:, j:j + 1],
                                     scale=lnw[:, j:j + 1]).then_inc(lth_ok, 1)
            with act.Fori(1, KT) as m:
                gates(m)

            for t in range(TT):
                act.wait_ge(x2_ok, 4 * (t + 1))
                if t:
                    act.wait_ge(sq_ok, TT + t)
                nc.scalar.activation(orow, x2[:, t, :], ACT.Square, accum_out=ss[:, t:t + 1]).then_inc(sq_ok, 1)
            for t in range(TT):
                act.wait_ge(h2T_pe, t + 1)
                if t >= 2:
                    act.wait_ge(lg_pe, t - 1)
                for b in range(2):
                    nc.scalar.activation(h2T[:, t % 2, 4 * b:4 * b + 4, :].rearrange("p k n -> p (k n)"), ps[:, 4 + b, :],
                                         ACT.Copy).then_inc(h2T_ok, 1)
            for t in range(TT):
                act.wait_ge(ntop_ok, t + 1)
                nc.scalar.activation(ew[:, t, :], top[:, t, 0:TOPK], ACT.Exp, bias=ntop[:, t:t + 1],
                                     accum_out=esum[:, t:t + 1]).then_inc(exw_ok, 1)

            act.wait_ge(tab_ok, 4)
            items = act.value_load(ntot[0:1, 0:1], min_val=NE, max_val=MAXI)
            final = act.value_load(ntot[0:1, 1:2], min_val=NE - 1, max_val=MAXI - 1)

            def rows_of(i, first=False):
                act.wait_ge(to_pe, i + 1)
                if not first:
                    act.wait_ge(orow_out, 16 * i)
                for b in range(2):
                    nc.scalar.activation(orow[0:SLOTS, 512 * b:512 * (b + 1)], ps[0:SLOTS, 4 + b, :], ACT.Copy).then_inc(orow_ok, 1)
                act.wait_ge(orow_ok, 2 * i + 2)
                act.dma_start(item_rows[bass.ds(i * SLOTS, SLOTS), :], orow[0:SLOTS, :]).then_inc(orow_out, 16)

            def tanhs(i):
                for half in range(2):
                    act.wait_ge(act_ok, 10 * i + 5 * half + 2)
                    nc.scalar.activation(tsb[:, 4 * half:4 * half + 4, :].rearrange("p k n -> p (k n)"),
                                         gsb[:, 4 * half:4 * half + 4, :].rearrange("p k n -> p (k n)"),
                                         ACT.Tanh, scale=0.5 * ALPHA).then_inc(tan_ok, 1)

            def tokens_in(i, first=False):
                act.wait_ge(tx_pe, i + 1)
                if not first:
                    act.wait_ge(gu_pe, 9 * i)
                for b in range(2):
                    nc.scalar.activation(xT[:, 4 * b:4 * b + 4, :].rearrange("p k n -> p (k n)"), ps[:, 4 + b, 0:4 * SLOTS],
                                         ACT.Copy).then_inc(xTi_ok, 1)

            tokens_in(0, first=True)
            tanhs(0)
            tokens_in(1)
            rows_of(0, first=True)
            with act.Fori(1, final) as i:
                tanhs(i)
                tokens_in(i + 1)
                rows_of(i)
            tanhs(final)
            tokens_in(items)
            rows_of(final)
            for t in range(TT):
                act.wait_ge(fin_ok, 6 * t + 5)
                if t:
                    act.wait_ge(sq_ok, 2 * TT + t)
                nc.scalar.activation(orow, x2[:, t, :], ACT.Square, accum_out=ss[:, t:t + 1]).then_inc(sq_ok, 1)
            plain(nc.scalar, orow_out, 16 * items, x_in, 16)

        @block.vector
        def _(dve):
            V = nc.vector
            dve.wait_ge(prT_ok, 1)
            V.tensor_scalar(ctmp[:, :], ps[:, 6, 0:KT], 0.5, None, ALU.mult).then_inc(par_ok, 1)
            dve.wait_ge(cact_t, 1)
            V.scalar_tensor_tensor(cact[:, :], cact[:, :], 1.0, ctmp[:, :], ALU.add, ALU.mult).then_inc(cact_ok, 1)
            dve.wait_ge(rstd_ok, 1)
            for t in range(TT):
                V.tensor_scalar(xs[:, t, :], xs[:, t, :], rstd[:, t:t + 1], None, ALU.mult).then_inc(xn_ok, 1)
            dve.wait_ge(prT_ok, 2)
            cw = ps[:, 4, 0:P].rearrange("p (k t) -> p k t", k=TAPS)
            cb = ps[:, 4, 384:384 + 80]
            for k in range(TAPS):
                V.tensor_scalar(ptab[:, :, 4 * k:4 * k + 2], cw[:, k, 0:16].rearrange("p (g a) -> p g a", a=2), 0.5, None,
                                ALU.mult).then_inc(par_ok, 1)
            V.tensor_scalar(ptab[:, :, 2:16:4], cw[:, :, 16:24].rearrange("p k g -> p g k"), 0.5, None, ALU.mult).then_inc(par_ok, 1)
            V.tensor_scalar(ptab[:, :, 3:16:4], cw[:, :, 24:32].rearrange("p k g -> p g k"), 0.5, None, ALU.mult).then_inc(par_ok, 1)
            V.tensor_scalar(ptab[:, :, 16:18], cb[:, 0:16].rearrange("p (g a) -> p g a", a=2), 0.5, None, ALU.mult).then_inc(par_ok, 1)
            V.tensor_scalar(ptab[:, :, 18:20], cb[:, 16:32].rearrange("p (a g) -> p g a", a=2), 0.5, None, ALU.mult).then_inc(par_ok, 1)
            V.tensor_scalar(ptab[:, :, CW:CW + CTAPS], ps[:, 4, P:P + CTAPS * G].rearrange("p (k g) -> p g k", g=G), 0.5, None,
                            ALU.mult).then_inc(par_ok, 1)
            V.tensor_copy(ptab[:, :, PW - 1], cb[:, 32:40]).then_inc(par_ok, 1)
            V.tensor_scalar(lnw[:, :], cb[:, 40:48], 0.5, None, ALU.mult).then_inc(par_ok, 1)
            V.tensor_scalar(lnb[:, :], cb[:, 48:56], 0.5, None, ALU.mult).then_inc(par_ok, 1)
            V.tensor_copy(n1w[:, :], cb[:, 56:64]).then_inc(par_ok, 1)
            V.tensor_copy(snw[:, :], cb[:, 64:80]).then_inc(par_ok, 1)
            dve.wait_ge(prT_ok, 4)
            V.tensor_copy(badaT[:, :], ps[:, 5, 0:VPT]).then_inc(par_ok, 1)
            V.tensor_copy(bdn[:, :], ps[:, 5, P:3 * P]).then_inc(par_ok, 1)
            V.tensor_copy(bgu[:, :, :].rearrange("p a b -> p (a b)"), ps[:, 6, :]).then_inc(par_ok, 1)
            dve.wait_ge(modT_pe, 1)
            dve.wait_ge(par_ok, 18)
            V.tensor_tensor(mod[:, :], ps[:, 7, 0:VPT], badaT[:, :], ALU.add).then_inc(mod_ok, 1)
            V.memset(raw[:, :, 0:TAPS - 1], 0.0).then_inc(pads_ok, 1)
            V.memset(upad[:, 0:CTAPS - 1], 0.0).then_inc(pads_ok, 1)
            dve.wait_ge(mod_ok, 1)
            V.scalar_tensor_tensor(a1[:, :], mod[:, KT:2 * KT], 1.0, n1w[:, :], ALU.add, ALU.mult).then_inc(a1_ok, 1)

            dve.wait_ge(dtr_ok, 1)
            dve.wait_ge(bc_in, 64)
            V.tensor_tensor(dt[:, :, :], ps[:, 4, 0:P].rearrange("p (t h) -> p t h", t=TT),
                            dtb.unsqueeze(1).to_broadcast([P, TT, H]), ALU.add).then_inc(time_dve, 1)
            dve.wait_ge(time_dve, 1)
            V.scalar_tensor_tensor(adt[:, :, :], dt[:, :, :], -1.0, dt[:, :, :], ALU.mult, ALU.max).then_inc(time_dve, 1)
            dve.wait_ge(time_act, 2)
            V.scalar_tensor_tensor(dt[:, :, :], dt[:, :, :], 0.0, eacs[:, :, :], ALU.max, ALU.add).then_inc(time_dve, 1)
            dve.wait_ge(time_dve, 3)
            dve.wait_ge(time_act, 3)
            V.scalar_tensor_tensor(adt[:, :, :], dt[:, :, :], -1.0, aneg.unsqueeze(1).to_broadcast([P, TT, H]),
                                   ALU.mult, ALU.mult).then_inc(time_dve, 1)
            dve.wait_ge(acs_pe, 1)
            V.tensor_copy(acs[:, :, :].rearrange("p t h -> p (t h)"), ps[:, 5, 0:P]).then_inc(time_dve, 1)
            V.tensor_copy(junk[0:H, 0:S], ps[0:H, 6, :]).then_inc(time_dve, 1)
            dve.wait_ge(time_dve, 5)
            dve.wait_ge(time_act, 5)
            V.tensor_tensor(dte[:, :, :].rearrange("p t h -> p (t h)"), ps[:, 5, P:2 * P],
                            acs[:, :, :].rearrange("p t h -> p (t h)"), ALU.subtract).then_inc(time_dve, 1)

            def params(g, first=False):
                if not first:
                    dve.wait_ge(c31_ok, 32 * g)
                V.tensor_copy(pcur[:, :], ptab[:, bass.ds(g, 1), :].rearrange("p a b -> p (a b)")).then_inc(pcur_ok, 1)

            def conv(g, j0, first=False):
                n = 16 * g + 4 * j0
                dve.wait_ge(pcur_ok, g + 1)
                dve.wait_ge(raw_bc if j0 else raw_x, 2 * g + 2)
                if not first:
                    dve.wait_ge(cv_ok, 4 * g)
                for k in range(TAPS):
                    for j in (j0, j0 + 1):
                        src = raw[:, j, k:k + S]
                        w = pcur[:, 4 * k + j:4 * k + j + 1]
                        if k == 0:
                            V.tensor_scalar(cacc[:, j, :], src, w, pcur[:, 16 + j:17 + j], ALU.mult, ALU.add).then_inc(conv_ok, 1)
                        else:
                            dve.wait_ge(conv_ok, n + 2 * k + (j - j0) - 1)
                            V.scalar_tensor_tensor(cacc[:, j, :], src, w, cacc[:, j, :], ALU.mult, ALU.add).then_inc(conv_ok, 1)

            def conv_silu(g, first=False):
                for j in range(4):
                    dve.wait_ge(ctan_ok, 4 * g + j + 1)
                    if not first:
                        dve.wait_ge(Y_ok, 4 * g)
                    V.scalar_tensor_tensor(cv[:, j, :], ctan[:, j, :], 1.0, cacc[:, j, :], ALU.add, ALU.mult).then_inc(cv_ok, 1)

            def glu(g, first=False):
                dve.wait_ge(gtan_ok, g + 1)
                if first:
                    dve.wait_ge(pads_ok, 2)
                else:
                    dve.wait_ge(c31_ok, 32 * g)
                V.scalar_tensor_tensor(upad[:, CTAPS - 1:], ugate, 1.0, ps[:, 0, :], ALU.add, ALU.mult).then_inc(glu_ok, 1)

            def taps31(g, lo, hi):
                for k in range(lo, hi):
                    if k == 0:
                        dve.wait_ge(glu_ok, g + 1)
                        dve.wait_ge(time_dve, 6)
                        dve.wait_ge(side_out, 16)
                        V.tensor_scalar(c31[:, 0, :], upad[:, 0:S], pcur[:, CW:CW + 1], pcur[:, PW - 1:PW], ALU.mult,
                                        ALU.add).then_inc(c31_ok, 1)
                    elif k == 1:
                        V.tensor_scalar(c31[:, 1, :], upad[:, 1:1 + S], pcur[:, CW + 1:CW + 2], None, ALU.mult).then_inc(c31_ok, 1)
                    elif k < CTAPS:
                        dve.wait_ge(c31_ok, 32 * g + k - 1)
                        V.scalar_tensor_tensor(c31[:, k % 2, :], upad[:, k:k + S], pcur[:, CW + k:CW + k + 1], c31[:, k % 2, :],
                                               ALU.mult, ALU.add).then_inc(c31_ok, 1)
                    else:
                        dve.wait_ge(c31_ok, 32 * g + CTAPS)
                        V.tensor_tensor(uT[:, bass.ds(g, 1), :].rearrange("p a b -> p (a b)"), c31[:, 0, :], c31[:, 1, :],
                                        ALU.add).then_inc(c31_ok, 1)

            def z_silu(g, first=False):
                for b in range(2):
                    dve.wait_ge(ztan_ok, 2 * g + b + 1)
                    if not first:
                        dve.wait_ge(y_ok, 14 * g)
                    V.scalar_tensor_tensor(zs[:, 2 * b:2 * b + 2, :].rearrange("p a b -> p (a b)"),
                                           ztan[:, :, :].rearrange("p a b -> p (a b)"), 1.0, ps[:, 2 + b, :],
                                           ALU.add, ALU.mult).then_inc(zs_ok, 1)

            def segments(g, c, first):
                if c == 0:
                    if not first:
                        dve.wait_ge(seg_ok, 16 * g)
                    V.tensor_copy(acsc[:, :, :], acs[:, :, bass.ds(g * HG, HG)]).then_inc(acsc_ok, 1)
                    dve.wait_ge(acsc_ok, g + 1)
                    dve.wait_ge(dec_in, 16 * (g + 1))
                if not first or c >= 2:
                    dve.wait_ge(m_ok, 4 * g + c - 1)
                for h in range(HG):
                    V.tensor_scalar(seg[:, c % 2, h, :], dec[:, h, ch(c)], acsc[:, c, h:h + 1], 0.0, ALU.subtract,
                                    ALU.min).then_inc(seg_ok, 1)

            def mix(g, c, first):
                dve.wait_ge(CB_ok, 4 * g + c + 1)
                if not first or c:
                    dve.wait_ge(m_ok, 4 * g + c)
                V.tensor_tensor(cbm[:, :], ps[:, 5, 0:P], tri[:, :], ALU.mult).then_inc(cbm_ok, 1)
                dve.wait_ge(cbm_ok, 4 * g + c + 1)
                dve.wait_ge(exp_ok, 4 * g + c + 1)
                if not first or c >= 2:
                    dve.wait_ge(Y_ok, 4 * g + c - 1)
                V.tensor_tensor(mm[:, c % 2], seg[:, c % 2], cbm[:, :].unsqueeze(1).to_broadcast([P, HG, P]),
                                ALU.mult).then_inc(m_ok, 1)

            def heads(t, g, c):
                return t[:, c, bass.ds(g * HG, HG)].unsqueeze(2).to_broadcast([P, HG, HD])

            def h4(v):
                return v.rearrange("p (h d) -> p h d", h=HG)

            def states(g, c, first):
                new = h4(ps[:, 5, P:P + GW])
                if c == 0:
                    dve.wait_ge(ST_ok, 3 * g + 1)
                    if not first:
                        dve.wait_ge(Y_ok, 4 * g)
                    V.tensor_copy(state[:, :, :], new).then_inc(state_ok, 1)
                    return
                dve.wait_ge(Y_ok, 4 * g + c + 1)
                dve.wait_ge(state_ok, 5 * g + STATE_AFTER[c - 1])
                V.tensor_tensor(state[:, :, :], state[:, :, :], heads(cdec, g, c), ALU.mult).then_inc(state_ok, 1)
                dve.wait_ge(ST_ok, 3 * g + c + 1)
                dve.wait_ge(state_ok, 5 * g + STATE_AFTER[c] - 1)
                V.tensor_tensor(state[:, :, :], state[:, :, :], new, ALU.add).then_inc(state_ok, 1)

            def outputs(g, c, first):
                n = y_after(g, c) - (2 if c == 0 else 4)
                dve.wait_ge(Y_ok, 4 * g + c + 1)
                if not first or c:
                    dve.wait_ge(y_ok, n)
                diag = ps[:, 6, 0:GW]
                if c:
                    V.tensor_tensor(h4(ytmp[:, :]), h4(ps[:, 6, GW:2 * GW]), heads(eacs, g, c), ALU.mult).then_inc(y_ok, 1)
                    dve.wait_ge(y_ok, n + 1)
                    V.tensor_tensor(ytmp[:, :], ytmp[:, :], diag, ALU.add).then_inc(y_ok, 1)
                    dve.wait_ge(y_ok, n + 2)
                    diag = ytmp[:, :]
                    n += 2
                dve.wait_ge(xdd_ok, 4 * g + c + 1)
                V.tensor_tensor(ytmp[:, :], diag, xdd[:, c % 2].rearrange("p h d -> p (h d)"), ALU.add).then_inc(y_ok, 1)
                dve.wait_ge(y_ok, n + 1)
                dve.wait_ge(zs_ok, 2 * g + 2)
                if not first:
                    dve.wait_ge(YT_ok, 2 * g - 1 + c // 2)
                V.tensor_tensor(yg[:, c, :], ytmp[:, :], zs[:, c, :], ALU.mult).then_inc(y_ok, 1)

            def normalise(g, r):
                dve.wait_ge(yrstd_ok, 2 * g + r + 1)
                for c in (2 * r, 2 * r + 1):
                    V.tensor_scalar(yg[:, c, :], yg[:, c, :], rstd[:, TT + c:TT + c + 1], None, ALU.mult).then_inc(ysc_ok, 1)

            params(0, first=True)
            conv(0, 0, first=True)
            conv(0, 2, first=True)
            glu(0, first=True)
            taps31(0, 0, 32)
            z_silu(0, first=True)

            def group(g, first=False, last=False):
                if not first:
                    normalise(g - 1, 1)
                conv_silu(g, first)
                segments(g, 0, first)
                mix(g, 0, first)
                if not last:
                    params(g + 1)
                    conv(g + 1, 0)
                segments(g, 1, first)
                states(g, 0, first)
                outputs(g, 0, first)
                mix(g, 1, first)
                if not last:
                    conv(g + 1, 2)
                segments(g, 2, first)
                states(g, 1, first)
                outputs(g, 1, first)
                mix(g, 2, first)
                if not last:
                    glu(g + 1)
                    taps31(g + 1, 0, 16)
                normalise(g, 0)
                segments(g, 3, first)
                states(g, 2, first)
                outputs(g, 2, first)
                mix(g, 3, first)
                if not last:
                    taps31(g + 1, 16, 27)
                dve.wait_ge(ada_l, 2 * g + 2)
                dve.wait_ge(arow_in, 16 * g + 16)
                V.tensor_tensor(arow, arow, ps[0:1, 1, :], ALU.add).then_inc(arow_ok, 1)
                if not last:
                    taps31(g + 1, 27, 32)
                outputs(g, 3, first)
                if not last:
                    z_silu(g + 1)

            group(0, first=True)
            with dve.Fori(1, G - 1) as g:
                group(g)
            group(G - 1, last=True)
            normalise(G - 1, 1)

            dve.wait_ge(mean_pe, 1)
            for j in range(KT):
                V.tensor_tensor(uT[:, j, :], uT[:, j, :], ps[:, 4, :], ALU.subtract).then_inc(cen_ok, 1)
            dve.wait_ge(lsd_ok, 1)
            V.reciprocal(lrs, lrs).then_inc(lrs_ok, 1)
            dve.wait_ge(lrs_ok, 1)
            for j in range(KT):
                V.tensor_tensor(uT[:, j, :], uT[:, j, :], lrs, ALU.mult).then_inc(lnm_ok, 1)
            for j in range(KT):
                dve.wait_ge(lnm_ok, j + 1)
                V.tensor_scalar(lv[:, j % 2, :], uT[:, j, :], lnw[:, j:j + 1], lnb[:, j:j + 1], ALU.mult, ALU.add).then_inc(lnv_ok, 1)
                dve.wait_ge(lnv_ok, j + 1)
                dve.wait_ge(lth_ok, j + 1)
                V.scalar_tensor_tensor(uT[:, j, :], lth[:, j % 2, :], 1.0, lv[:, j % 2, :], ALU.add, ALU.mult).then_inc(u_ok, 1)

            def merge(m):
                dve.wait_ge(gat_ok, m + 1)
                dve.wait_ge(ya_pe, m + 1)
                if not isinstance(m, int):
                    dve.wait_ge(mrg_ok, 3 * m)
                V.scalar_tensor_tensor(m1[:, 0, :], gt[:, 0, :], 1.0, ps[:, 2, :], ALU.add, ALU.mult).then_inc(mrg_ok, 1)
                dve.wait_ge(gbt_ok, m + 1)
                dve.wait_ge(yb_pe, m + 1)
                V.scalar_tensor_tensor(m1[:, 1, :], gt[:, 1, :], 1.0, ps[:, 3, :], ALU.add, ALU.mult).then_inc(mrg_ok, 1)
                dve.wait_ge(mrg_ok, 3 * m + 2)
                V.tensor_tensor(mT[:, bass.ds(m, 1), :].rearrange("p a b -> p (a b)"), m1[:, 0, :], m1[:, 1, :],
                                ALU.add).then_inc(mrg_ok, 1)

            merge(0)
            with dve.Fori(1, KT) as m:
                merge(m)

            dve.wait_ge(brow_in, 80)
            V.tensor_scalar(g1row, g1row, 0.5, None, ALU.mult).then_inc(row_ok, 1)
            V.scalar_tensor_tensor(a2row, a2row, 1.0, h2[:, 0, :], ALU.add, ALU.mult).then_inc(row_ok, 1)
            dve.wait_ge(row_ok, 2)
            dve.wait_ge(x2_in, 16)

            def second_norm(t):
                dve.wait_ge(rstd_ok, t + 2)
                if t >= 2:
                    dve.wait_ge(hrow_out[t % 2], 16)
                    dve.wait_ge(h2T_pe, t - 1)
                V.scalar_tensor_tensor(h2[:, t % 2, :], x2[:, t, :], rstd[:, t:t + 1], a2row, ALU.mult, ALU.mult).then_inc(h2_ok, 1)
                dve.wait_ge(h2_ok, 2 * t + 1)
                V.tensor_tensor(h2[:, t % 2, :], h2[:, t % 2, :], s2row, ALU.add).then_inc(h2_ok, 1)

            for t in range(TT):
                for hf in range(2):
                    n = 2 * t + hf
                    dve.wait_ge(o_pe, n + 1)
                    if n:
                        dve.wait_ge(x2_ok, 2 * n)
                    V.tensor_tensor(junk[:, hf * 512:(hf + 1) * 512], ps[:, n % 4, :], g1row[:, hf * 512:(hf + 1) * 512],
                                    ALU.mult).then_inc(x2_ok, 1)
                    dve.wait_ge(x2_ok, 2 * n + 1)
                    V.tensor_tensor(x2[:, t, hf * 512:(hf + 1) * 512], x2[:, t, hf * 512:(hf + 1) * 512],
                                    junk[:, hf * 512:(hf + 1) * 512], ALU.add).then_inc(x2_ok, 1)
                if t:
                    second_norm(t - 1)
            second_norm(TT - 1)

            done = [0]

            def link(ins):
                done[0] += 1
                ins.then_inc(rt_ok, 1)
                dve.wait_ge(rt_ok, done[0])

            for t in range(TT):
                dve.wait_ge(lg_pe, t + 1)
                link(V.tensor_tensor(lg[:, t, :], ps[:, LG_BANK[t], 0:NE], brow[:, :], ALU.add))
                link(V.max(top[:, t, :], lg[:, t, :]))
                V.tensor_scalar(ntop[:, t:t + 1], top[:, t, 0:1], -1.0, None, ALU.mult).then_inc(ntop_ok, 1)
                link(V.max_index(topi[:, t, :], top[:, t, :], lg[:, t, :]))
                link(V.tensor_copy(topf[:, t, :], topi[:, t, :]))
                for k in range(TOPK):
                    link(V.tensor_scalar(oh[:, t, k, :], io32[:, :], topf[:, t, k:k + 1], None, ALU.is_equal))
                V.tensor_reduce(mask[:, t, :], oh[:, t].rearrange("p k e -> p e k"), AX.X, ALU.add).then_inc(mask_ok, 1)
            dve.wait_ge(exw_ok, TT)
            link(V.reciprocal(esum[:, :], esum[:, :]))
            for t in range(TT):
                link(V.tensor_scalar(tw[:, t, :], ew[:, t, :], esum[:, t:t + 1], None, ALU.mult))
            dve.wait_ge(rank_pe, 1)
            dve.wait_ge(mask_ok, TT)
            f = "p t n -> p (t n)"
            link(V.tensor_copy(pos.rearrange(f), ps[:, 2, 0:TT * NE]))
            link(V.tensor_copy(cnt, ps[:, 2, TT * NE:(TT + 1) * NE]))
            link(V.tensor_scalar(ci, pos, float(SLOTS), None, ALU.is_ge))
            link(V.tensor_scalar(more, cnt, float(SLOTS), None, ALU.is_gt))
            for j in range(2, MOREMAX + 1):
                link(V.scalar_tensor_tensor(ci, pos, float(SLOTS * j), ci, ALU.is_ge, ALU.add))
                link(V.scalar_tensor_tensor(more, cnt, float(SLOTS * j), more, ALU.is_gt, ALU.add))
            link(V.tensor_tensor_scan(incl, ones[:, 0:NE], more, 0.0, ALU.mult, ALU.add))
            link(V.tensor_tensor(excl, incl, more, ALU.subtract))
            io = io32[:, :].unsqueeze(1).to_broadcast([P, TT, NE])
            link(V.tensor_tensor(r1, ci, excl.unsqueeze(1).to_broadcast([P, TT, NE]), ALU.add))
            link(V.scalar_tensor_tensor(r1, r1, float(NE - 1), io, ALU.add, ALU.subtract))
            link(V.tensor_scalar(r2, ci, 0.0, None, ALU.is_gt))
            link(V.tensor_tensor(r1, r1, r2, ALU.mult))
            link(V.tensor_tensor(r1, r1, io, ALU.add))
            link(V.scalar_tensor_tensor(r2, ci, -float(SLOTS), pos, ALU.mult, ALU.add))
            link(V.scalar_tensor_tensor(slot[:, :, :], r1, float(SLOTS), r2, ALU.mult, ALU.add))
            for t in range(TT):
                link(V.tensor_tensor(oh[:, t], oh[:, t], slot[:, t, :].unsqueeze(1).to_broadcast([P, TOPK, NE]), ALU.mult))
                link(V.tensor_reduce(slotk[:, t, :], oh[:, t], AX.X, ALU.add))
            V.tensor_copy(slotki[:, :], slotk[:, :, :].rearrange("p t k -> p (t k)")).then_inc(tab_ok, 1)
            link(V.scalar_tensor_tensor(slot[:, :, :], slot[:, :, :], 1.0, mask[:, :, :], ALU.add, ALU.mult))
            link(V.tensor_scalar(slot[:, :, :], slot[:, :, :], -1.0, None, ALU.add))
            link(V.tensor_tensor(cmp, incl[0:1, :].unsqueeze(1).to_broadcast([1, MAXI + 1 - NE, NE]),
                                 io32[0:1, 0:MAXI + 1 - NE].unsqueeze(2).to_broadcast([1, MAXI + 1 - NE, NE]), ALU.is_le))
            link(V.tensor_copy(eidf[0:1, 0:NE], io32[0:1, :]))
            link(V.tensor_reduce(eidf[0:1, NE:], cmp, AX.X, ALU.add))
            link(V.tensor_scalar(eidf[0:1, :], eidf[0:1, :], float(NE - 1), None, ALU.min))
            V.tensor_copy(eid[0:1, :], eidf[0:1, :]).then_inc(tab_ok, 1)
            V.tensor_scalar(ntot[0:1, 0:1], incl[0:1, NE - 1:NE], float(NE), None, ALU.add).then_inc(tab_ok, 1)
            V.tensor_scalar(ntot[0:1, 1:2], incl[0:1, NE - 1:NE], float(NE - 1), None, ALU.add).then_inc(tab_ok, 1)
            dve.wait_ge(tab_ok, 4)
            items = dve.value_load(ntot[0:1, 0:1], min_val=NE, max_val=MAXI)

            def select(i, e, first=False):
                if not first:
                    dve.wait_ge(tok_pe, i)
                V.tensor_scalar(rel[:, :], slot[:, :, bass.ds(e, 1)].rearrange("p t a -> p (t a)"), ibase[:, bass.ds(i, 1)], None,
                                ALU.subtract).then_inc(sel_ok, 1)
                dve.wait_ge(sel_ok, 5 * i + 1)
                for t in range(TT):
                    V.tensor_scalar(sel[:, t, :], io96[:, :], rel[:, t:t + 1], None, ALU.is_equal).then_inc(sel_ok, 1)
                dve.wait_ge(tok_pe, i + 1)
                if not first:
                    dve.wait_ge(xg_in, 16 * i)
                V.tensor_copy(tok[0:SLOTS, :], ps[0:SLOTS, 7, 500:501]).then_inc(tok_ok, 1)

            def swiglu(i, e, half):
                n = 10 * i + 5 * half
                ks = slice(4 * half, 4 * half + 4)
                g_, l_, t_, h_ = gsb[:, ks, :], lsb[:, ks, :], tsb[:, ks, :], hid[:, ks, :]

                def bias(j):
                    return bgu[:, j, bass.ds(e * KT + 4 * half, 4)].unsqueeze(2).to_broadcast([P, 4, SLOTS])

                def acc(b):
                    return ps[:, b, 0:4 * SLOTS].rearrange("p (k n) -> p k n", k=4)

                dve.wait_ge(gu_pe, 9 * i + 8 + half)
                V.tensor_tensor(g_, acc(half), bias(0), ALU.add).then_inc(act_ok, 1)
                dve.wait_ge(act_ok, n + 1)
                V.tensor_scalar(g_, g_, LIMIT, None, ALU.min).then_inc(act_ok, 1)
                V.tensor_tensor(l_, acc(2 + half), bias(1), ALU.add).then_inc(act_ok, 1)
                dve.wait_ge(act_ok, n + 3)
                V.tensor_scalar(l_, l_, LIMIT, -LIMIT, ALU.min, ALU.max).then_inc(act_ok, 1)
                dve.wait_ge(tan_ok, 2 * i + half + 1)
                V.scalar_tensor_tensor(g_, t_, 1.0, g_, ALU.add, ALU.mult).then_inc(act_ok, 1)
                dve.wait_ge(act_ok, n + 5)
                V.scalar_tensor_tensor(h_, l_, 1.0, g_, ALU.add, ALU.mult).then_inc(hid_ok, 1)

            def results(i, e, first=False):
                dve.wait_ge(dn_pe, 8 * i + 8)
                if not first:
                    dve.wait_ge(to_pe, i)
                for b in range(2):
                    V.scalar_tensor_tensor(oT[:, 4 * b:4 * b + 4, :], ps[:, 6 + b, 0:4 * SLOTS].rearrange("p (k n) -> p k n", k=4), 0.5,
                                           bdn[:, bass.ds(e * KT + 4 * b, 4)].unsqueeze(2).to_broadcast([P, 4, SLOTS]),
                                           ALU.mult, ALU.add).then_inc(oT_ok, 1)

            select(0, 0, first=True)
            select(1, 1)
            swiglu(0, 0, 0)
            swiglu(0, 0, 1)
            results(0, 0, first=True)
            with dve.Fori(1, items) as i:
                e_next = dve.value_load(eid[0:1, bass.ds(i + 1, 1)], min_val=0, max_val=NE - 1)
                select(i + 1, e_next)
                e = dve.value_load(eid[0:1, bass.ds(i, 1)], min_val=0, max_val=NE - 1)
                swiglu(i, e, 0)
                swiglu(i, e, 1)
                results(i, e)

            dve.wait_ge(fn_in, 16)
            for t in range(TT):
                n = 6 * t
                dve.wait_ge(got_in[t], 16 * TOPK)
                acc = got[:, t * TOPK, :]
                V.tensor_scalar(acc, acc, tw[:, t, 0:1], None, ALU.mult).then_inc(fin_ok, 1)
                for k in range(1, TOPK):
                    dve.wait_ge(fin_ok, n + k)
                    V.scalar_tensor_tensor(acc, got[:, t * TOPK + k, :], tw[:, t, k:k + 1], acc, ALU.mult,
                                           ALU.add).then_inc(fin_ok, 1)
                dve.wait_ge(fin_ok, n + 4)
                link(V.tensor_tensor(acc, acc, g2row, ALU.mult))
                V.tensor_tensor(x2[:, t, :], x2[:, t, :], acc, ALU.add).then_inc(fin_ok, 1)
                dve.wait_ge(rstd_ok, TT + t + 2)
                V.scalar_tensor_tensor(x2[:, t, :], x2[:, t, :], rstd[:, t:t + 1], fn, ALU.mult, ALU.mult).then_inc(fin_ok, 1)

        @block.tensor
        def _(pe):
            T = nc.tensor
            pe.wait_ge(const_ok, 11)
            pe.wait_ge(once_in, 16)
            T.transpose(ps[:, 6, 0:KT], prow[0:KT, 7, :], ident[0:KT, 0:KT]).then_inc(prT_ok, 1)

            def acc_k(out_, lhs, rhs, n=KT):
                for k in range(n):
                    last = T.matmul(out_, lhs(k), rhs(k), start=(k == 0), stop=(k == n - 1))
                return last

            pe.wait_ge(cact_ok, 1)
            for s in range(8):
                pe.wait_ge(ada_in[s], 16)
                acc_k(ps[0:1, s // 2, (s % 2) * 256:(s % 2 + 1) * 256], lambda k: cact[:, k:k + 1],
                      lambda k: ada[:, s, k, :]).then_inc(ada_ok, 1)
            pe.wait_ge(rows_in, 12 * 16)
            n2 = CTAPS * G - P
            T.transpose(ps[:, 4, 0:P], prow[:, 0, :], ident[:, :])
            T.transpose(ps[:, 4, P:2 * P], prow[:, 1, :], ident[:, :])
            T.transpose(ps[:, 4, 2 * P:2 * P + n2], prow[0:n2, 2, :], ident[0:n2, 0:n2])
            T.transpose(ps[:, 4, 384:384 + 80], prow[0:80, 3, :], ident[0:80, 0:80]).then_inc(prT_ok, 1)
            T.transpose(ps[:, 5, 0:VPT], prow[0:VPT, 4, :], ident[0:VPT, 0:VPT])
            T.transpose(ps[:, 5, P:2 * P], prow[:, 5, :], ident[:, :])
            T.transpose(ps[:, 5, 2 * P:3 * P], prow[:, 6, :], ident[:, :]).then_inc(prT_ok, 1)
            for j in range(2):
                for s in range(2):
                    last = T.transpose(ps[:, 6, (2 * j + s) * P:(2 * j + s + 1) * P], browg[:, s, j::2], ident[:, :])
            last.then_inc(prT_ok, 1)

            pe.wait_ge(cact_t, 5)
            for j in range(VPT):
                last = T.matmul(ps[:, 7, j:j + 1], modrow[0:1, j * P:(j + 1) * P], ones[0:1, 0:1], start=True, stop=True)
            last.then_inc(modT_pe, 1)
            for k in range(KT):
                for t in range(TT):
                    pe.wait_ge(xn_ok, t + 1)
                    if k >= 4:
                        pe.wait_ge(hT_ok, k - 3)
                    last = T.transpose(ps[:, k % 4, ch(t)], xs[:, t, k * P:(k + 1) * P], ident[:, :])
                last.then_inc(xT_ok, 1)
            pe.wait_ge(hT_ok, KT)
            pe.wait_ge(par_ok, 18)
            pe.wait_ge(wdt_in, 16)
            for t in range(TT):
                last = acc_k(ps[:, 4, t * H:(t + 1) * H], lambda k: hT[:, k, ch(t)], lambda k: wdt[:, k, :])
            last.then_inc(dtr_ok, 1)

            def project(b, w):
                return acc_k(ps[:, b, :], lambda k: wg[:, k, w:w + P], lambda k: hT[:, k, :])

            def project_x(g, first=False):
                pe.wait_ge(wx_in, 16 * (g + 1))
                if not first:
                    pe.wait_ge(glu_ok, g)
                    if not (isinstance(g, int) and g == 1):
                        pe.wait_ge(arow_ok, g - 1)
                for j in range(2):
                    project(j, W_X + j * P).then_inc(proj_x, 1)

            def project_bc(g, first=False):
                pe.wait_ge(wbc_in, 32 * (g + 1))
                if not first:
                    pe.wait_ge(zs_ok, 2 * g)
                project(2, W_B).then_inc(proj_bc, 1)
                project(3, W_C).then_inc(proj_bc, 1)

            def project_vg(g):
                pe.wait_ge(wvg_in, 32 * (g + 1))
                pe.wait_ge(raw_x, 2 * (g + 1))
                project(0, W_V).then_inc(proj_vg, 1)
                project(1, W_G).then_inc(proj_vg, 1)

            def project_z(g):
                pe.wait_ge(wz_in, 16 * (g + 1))
                pe.wait_ge(raw_bc, 2 * (g + 1))
                for t in range(TT):
                    last = acc_k(ps[:, 2 + t // 2, (t % 2) * GW:(t % 2 + 1) * GW], lambda k: hT[:, k, ch(t)],
                                 lambda k: wg[:, k, W_Z:W_Z + GW])
                    if t % 2:
                        last.then_inc(proj_z, 1)

            project_x(0, first=True)
            pe.wait_ge(time_dve, 4)
            for c in range(TT):
                T.matmul(ps[:, 5, c * H:(c + 1) * H], tri[:, :], adt[:, c, :], start=True, stop=True)
                T.matmul(ps[:, 5, P + c * H:P + (c + 1) * H], ones[:, :], adt[:, c, :], start=True, stop=True)
                last = T.matmul(ps[0:H, 6, ch(c)], adt[:, c, :], tri[:, :], start=True, stop=True)
            last.then_inc(acs_pe, 1)
            project_bc(0, first=True)
            project_vg(0)
            project_z(0)

            def turn(g, c, first):
                pe.wait_ge(cv_ok, 4 * g + 4)
                if not first or c:
                    pe.wait_ge(xb_ok, 4 * g + c)
                for j in range(3):
                    last = T.transpose(ps[:, 4, j * P:(j + 1) * P], cv[:, j, ch(c)], ident[:, :])
                last.then_inc(T_ok, 1)
                if c:
                    pe.wait_ge(state_ok, 5 * g + STATE_AFTER[c - 1])
                if not first or c:
                    pe.wait_ge(cbm_ok, 4 * g + c)
                T.matmul(ps[:, 5, 0:P], cv[:, 2, ch(c)], cv[:, 3, ch(c)], start=True, stop=True).then_inc(CB_ok, 1)

            def chunk(g, c, first):
                pe.wait_ge(m_ok, 4 * g + c + 1)
                pe.wait_ge(xdt_ok, 4 * g + c + 1)
                if not first or c:
                    pe.wait_ge(y_ok, y_after(g, c - 1) if c else 14 * g)
                for h in range(HG):
                    last = T.matmul(ps[:, 6, h * HD:(h + 1) * HD], mm[:, c % 2, h, :], xdt[:, c % 2, h, :], start=True, stop=True)
                if c:
                    pe.wait_ge(state_ok, 5 * g + STATE_AFTER[c - 1])
                    last = T.matmul(ps[:, 6, GW:2 * GW], cv[:, 3, ch(c)], state[:, :, :].rearrange("p h d -> p (h d)"),
                                    start=True, stop=True)
                last.then_inc(Y_ok, 1)
                if c < 3:
                    pe.wait_ge(xdec_ok, 3 * g + c + 1)
                    if not first or c:
                        pe.wait_ge(state_ok, 5 * g + (STATE_AFTER[c - 1] if c else 0))
                    T.matmul(ps[:, 5, P:P + GW], xb[:, c % 2, GW:GW + P], xdec[:, c % 2].rearrange("p h d -> p (h d)"),
                             start=True, stop=True).then_inc(ST_ok, 1)

            def turn_y(g, r, first=False):
                pe.wait_ge(ysc_ok, 4 * g + 2 * r + 2)
                if not (first and r == 0):
                    pe.wait_ge(yT_ok, 4 * g + 2 * r)
                for i in range(2):
                    for c in range(2):
                        last = T.transpose(ps[:, 7, i * GW + c * P:i * GW + (c + 1) * P], yg[:, 2 * r + c, i * P:(i + 1) * P],
                                           ident[:, :])
                last.then_inc(YT_ok, 1)

            def ada_rest(g, last):
                pe.wait_ge(gtan_ok, G if last else g + 2)
                for s in range(2):
                    pe.wait_ge(ada_in[s], 16 * (g + 2))
                    acc_k(ps[0:1, 1, s * 256:(s + 1) * 256], lambda k: cact[:, k:k + 1],
                          lambda k: ada[:, s, k, :]).then_inc(ada_l, 1)

            def merge_gate_a(m, first=False):
                pe.wait_ge(mw_ga, 16 * (m + 1))
                if first:
                    pe.wait_ge(glu_ok, G)
                else:
                    pe.wait_ge(gat_ok, m)
                acc_k(ps[:, 0, :], lambda k: wga[:, k, :], lambda k: hT[:, k, :]).then_inc(ga_pe, 1)

            def group(g, first=False, last=False):
                if not last:
                    project_x(g + 1)
                else:
                    merge_gate_a(0, first=True)
                if not first:
                    turn_y(g - 1, 1)
                turn(g, 0, first)
                if not last:
                    project_bc(g + 1)
                chunk(g, 0, first)
                turn(g, 1, first)
                if not last:
                    project_vg(g + 1)
                chunk(g, 1, first)
                turn(g, 2, first)
                if not last:
                    project_z(g + 1)
                turn_y(g, 0, first)
                chunk(g, 2, first)
                turn(g, 3, first)
                ada_rest(g, last)
                chunk(g, 3, first)

            group(0, first=True)
            with pe.Fori(1, G - 1) as g:
                group(g)
            group(G - 1, last=True)
            turn_y(G - 1, 1)

            def gates(m, first=False):
                if not first:
                    merge_gate_a(m)
                pe.wait_ge(mw_gb, 16 * (m + 1))
                if not first:
                    pe.wait_ge(gbt_ok, m)
                acc_k(ps[:, 1, :], lambda k: wgb[:, k, :], lambda k: hT[:, k, :]).then_inc(gb_pe, 1)

            def branch_a(m, first=False):
                pe.wait_ge(mw_ya, 16 * (m + 1))
                if first:
                    pe.wait_ge(yT_ok, 4 * G)
                else:
                    pe.wait_ge(mrg_ok, 3 * m - 2)
                acc_k(ps[:, 2, :], lambda k: wya[:, k, :], lambda k: yT[:, k, :], 2 * KT).then_inc(ya_pe, 1)

            def branch_b(m, first=False):
                if first:
                    pe.wait_ge(u_ok, KT)
                else:
                    pe.wait_ge(mrg_ok, 3 * m - 1)
                pe.wait_ge(mw_yb, 16 * (m + 1))
                acc_k(ps[:, 3, :], lambda k: wyb[:, k, :], lambda k: uT[:, k, :]).then_inc(yb_pe, 1)

            pe.wait_ge(c31_ok, 32 * G)
            pe.wait_ge(xb_ok, 4 * G)
            acc_k(ps[:, 4, :], lambda k: mean_of[:, :], lambda k: uT[:, k, :]).then_inc(mean_pe, 1)
            pe.wait_ge(arow_ok, G)
            gates(0, first=True)
            branch_a(0, first=True)
            for j in range(KT):
                pe.wait_ge(lsq_ok, j + 1)
                T.matmul(ps[:, 5, :], mean_of[:, :], lsq[:, j % 2, :], start=(j == 0), stop=(j == KT - 1)).then_inc(var_pe, 1)
            gates(1)
            branch_b(0, first=True)
            with pe.Fori(1, KT - 1) as m:
                branch_a(m)
                branch_b(m)
                gates(m + 1)
            branch_a(KT - 1)
            branch_b(KT - 1)

            pe.wait_ge(wo_in, 16)
            pe.wait_ge(mrg_ok, 3 * KT)
            for t in range(TT):
                for hf in range(2):
                    n = 2 * t + hf
                    if n >= 4:
                        pe.wait_ge(x2_ok, 2 * (n - 4) + 1)
                    acc_k(ps[:, n % 4, :], lambda k: mT[:, k, ch(t)], lambda k: wo[:, k, hf * 512:(hf + 1) * 512]).then_inc(o_pe, 1)
            pe.wait_ge(once_in, 32)
            for t in range(TT):
                pe.wait_ge(h2_ok, 2 * (t + 1))
                if t:
                    pe.wait_ge(h2T_ok, 2 * t)
                for k in range(KT):
                    last = T.transpose(ps[:, 4 + k // 4, (k % 4) * P:(k % 4 + 1) * P], h2[:, t % 2, k * P:(k + 1) * P], ident[:, :])
                last.then_inc(h2T_pe, 1)
                pe.wait_ge(h2T_ok, 2 * t + 2)
                acc_k(ps[:, LG_BANK[t], 0:NE], lambda k: h2T[:, t % 2, k, :], lambda k: wr[:, k, :]).then_inc(lg_pe, 1)
            for t in range(TT + 1):
                o = ps[:, 2, t * NE:(t + 1) * NE]
                pe.wait_ge(mask_ok, min(t + 1, TT))
                for j in range(min(t, TT)):
                    last = T.matmul(o, ones[:, :], mask[:, j, :], start=(j == 0), stop=(t == TT and j == TT - 1))
                if t < TT:
                    T.matmul(o, before[:, :], mask[:, t, :], start=(t == 0), stop=True)
            last.then_inc(rank_pe, 1)

            pe.wait_ge(tab_ok, 4)
            items = pe.value_load(ntot[0:1, 0:1], min_val=NE, max_val=MAXI)

            def numbers(i, first=False):
                pe.wait_ge(sel_ok, 5 * (i + 1))
                if not first:
                    pe.wait_ge(tok_ok, i)
                acc_k(ps[0:SLOTS, 7, 500:501], lambda t: sel[:, t, :], lambda t: tid[:, t:t + 1], TT).then_inc(tok_pe, 1)

            def tokens_in(i, prev=None):
                pe.wait_ge(xg_in, 16 * (i + 1))
                if prev is not None:
                    pe.wait_ge(orow_ok, 2 * prev + 2)
                for k in range(KT):
                    last = T.transpose(ps[:, 4 + k // 4, (k % 4) * SLOTS:(k % 4 + 1) * SLOTS], xg[0:SLOTS, k * P:(k + 1) * P],
                                       ident[0:SLOTS, 0:SLOTS])
                last.then_inc(tx_pe, 1)

            def gate_up(i, ks):
                for k in ks:
                    pe.wait_ge(gu_in[k], 16 * (i + 1))
                    if k == 0:
                        pe.wait_ge(xTi_ok, 2 * i + 2)
                    for half in range(2):
                        for j in range(2):
                            for m in range(4 * half, 4 * half + 4):
                                last = T.matmul(ps[:, 2 * j + half, (m % 4) * SLOTS:(m % 4 + 1) * SLOTS],
                                                gu[:, k, j + 256 * m:256 * (m + 1):2], xT[:, k, :],
                                                start=(k == 0 and m % 4 == 0), stop=(k == KT - 1), skip_group_check=True)
                        if k == KT - 1 and half == 0:
                            last.then_inc(gu_pe, 1)
                    last.then_inc(gu_pe, 1)

            def down(i, first=False):
                for k in range(KT):
                    pe.wait_ge(dn_in[k], 16 * (i + 1))
                    if k == 0:
                        pe.wait_ge(hid_ok, 2 * i + 1)
                        pe.wait_ge(tok_ok, i + 2)
                        if not first:
                            pe.wait_ge(oT_ok, 2 * i)
                    if k == 4:
                        pe.wait_ge(hid_ok, 2 * i + 2)
                    for d in range(KT):
                        last = T.matmul(ps[:, 6 + d // 4, (d % 4) * SLOTS:(d % 4 + 1) * SLOTS], dn[:, k, d * P:(d + 1) * P],
                                        hid[:, k, :], start=(k == 0 and d % 4 == 0), stop=(k == KT - 1), skip_group_check=True)
                    last.then_inc(dn_pe, 1)

            def rows_of(i):
                pe.wait_ge(oT_ok, 2 * i + 2)
                pe.wait_ge(xTi_ok, 2 * (i + 2))
                for d in range(KT):
                    last = T.transpose(ps[0:SLOTS, 4 + d // 4, (d % 4) * P:(d % 4 + 1) * P], oT[:, d, :], ident[:, :])
                last.then_inc(to_pe, 1)

            numbers(0, first=True)
            tokens_in(0)
            gate_up(0, range(4))
            numbers(1)
            gate_up(0, range(4, KT))
            tokens_in(1)
            down(0, first=True)
            with pe.Fori(1, items) as i:
                gate_up(i, range(2))
                rows_of(i - 1)
                gate_up(i, range(2, 4))
                numbers(i + 1)
                gate_up(i, range(4, KT))
                tokens_in(i + 1, i - 1)
                down(i)
            rows_of(items - 1)


_INS = ["x", "c", "w_ada", "b_ada", "norm1_w", "w_in", "conv_ssm_w", "conv_ssm_b", "dt_bias", "a_log", "d_skip",
        "ssm_norm_w", "w_ssm_out", "conf_dw_w", "conf_dw_b", "conf_ln_w", "conf_ln_b", "w_conf_out", "w_o",
        "norm2_w", "w_router", "b_router", "w_gate_up", "b_gate_up", "w_down", "b_down", "final_norm_w"]
_OUTS = [((1, S, D), "float32")]


def kernel(**inputs):
    import numpy as _np
    import concourse.bacc as _bacc
    from concourse import mybir as _mybir
    from concourse.bass_utils import run_bass_kernel_spmd as _run

    nc = _bacc.Bacc("TRN2", target_bir_lowering=False, num_devices=1)
    arrays, args = {}, []
    for name in _INS:
        a = _np.ascontiguousarray(inputs[name])
        arrays[f"in_{name}_dram"] = a
        args.append(nc.dram_tensor(f"in_{name}_dram", a.shape, _mybir.dt.from_np(a.dtype), kind="ExternalInput").ap())
    for i, (shape, dtype) in enumerate(_OUTS):
        dt = _mybir.dt.from_np(_np.dtype(dtype))
        args.append(nc.dram_tensor(f"out_{i}_dram", shape, dt, kind="ExternalOutput").ap())
    build(nc, *args)
    r = _run(nc, [arrays], core_ids=[0])
    got = tuple(r.results[0][f"out_{i}_dram"] for i in range(len(_OUTS)))
    return got[0]
```
